# Optimizing a Trainium2 kernel written in Bass

```python
import jax, jax.numpy as jnp
from jax import lax
import numpy as np

D_MODEL = 1024
BATCH = 1
SEQ = 512
DEPTH = 2
DEC_BATCH = 8
DEC_SEQ = 8
PAST_LEN = 1024
PAGE_SIZE = 128

HEAD_DIM = 64
N_A_LAYERS = DEPTH // 2
N_B_LAYERS = DEPTH - N_A_LAYERS
MIX_WIDTH = 3 * D_MODEL // 4
RWKV_HEADS = MIX_WIDTH // HEAD_DIM
MEM_HEADS = 4
MEM_WIDTH = MEM_HEADS * HEAD_DIM
MEM_TOKENS = 256
DIL_GROUPS = ((128, 1), (512, 4), (2048, 16))
N_GROUPS = len(DIL_GROUPS)
GROUP_HEADS = MIX_WIDTH // (N_GROUPS * HEAD_DIM)
DIL_WIDTH = GROUP_HEADS * HEAD_DIM
D_FF = -(-8 * D_MODEL // (3 * 256)) * 256
LORA_W = 64
LORA_A = 64
LORA_V = 32
LORA_G = 128
ROPE_THETA = 10000.0
NORM_EPS = 1e-6
LNX_EPS = HEAD_DIM * 1e-5
Q_BLOCK = 128

kernel_name = 'rwkv7_dilated_yoco_decoder'

def rms_norm(x, g):
    xf = x.astype(jnp.float32)
    y = xf * lax.rsqrt(jnp.mean(xf * xf, axis=-1, keepdims=True) + NORM_EPS)
    return (y * g.astype(jnp.float32)).astype(x.dtype)

def rotary(x, pos):
    half = HEAD_DIM // 2
    inv = ROPE_THETA ** (-jnp.arange(half, dtype=jnp.float32) / half)
    ang = pos.astype(jnp.float32)[:, None] * inv[None, :]
    shp = (ang.shape[0],) + (1,) * (x.ndim - 3) + (half,)
    cos, sin = jnp.cos(ang).reshape(shp), jnp.sin(ang).reshape(shp)
    xf = x.astype(jnp.float32)
    x1, x2 = xf[..., :half], xf[..., half:]
    return jnp.concatenate([x1 * cos - x2 * sin, x2 * cos + x1 * sin], axis=-1).astype(x.dtype)

def mem_kv(mem, g, w):
    B, M, _ = mem.shape
    return (rms_norm(mem, g) @ w).reshape(B, M, 2, MEM_HEADS, HEAD_DIM)

def mem_attention(q, mk, mv):
    s = jnp.einsum('bthd,bmhd->bhtm', q, mk.astype(q.dtype)).astype(jnp.float32) * (HEAD_DIM ** -0.5)
    p = jax.nn.softmax(s, axis=-1).astype(mv.dtype)
    return jnp.einsum('bhtm,bmhd->bthd', p, mv)

def wkv7_scan(S0, r, w, k, v, kk, a):
    def step(S, inp):
        r_t, w_t, k_t, v_t, kk_t, a_t = inp
        sa = jnp.einsum('bhvk,bhk->bhv', S, -kk_t)
        S = (S * w_t[:, :, None, :] + sa[..., None] * (kk_t * a_t)[:, :, None, :]
             + v_t[..., None] * k_t[:, :, None, :])
        return S, jnp.einsum('bhvk,bhk->bhv', S, r_t)
    xs = tuple(jnp.moveaxis(t, 1, 0) for t in (r, w, k, v, kk, a))
    S, o = lax.scan(step, S0, xs)
    return S, jnp.moveaxis(o, 0, 1)

def rwkv7_layer(xn, shift0, S0, v_first, li, W):
    B, T, D = xn.shape
    f32 = jnp.float32
    x_prev = jnp.concatenate([shift0[:, None, :].astype(xn.dtype), xn[:, :-1]], axis=1)
    xx = x_prev - xn
    mu = W['a_mu'][li]
    xr, xw, xk, xv, xa, xg = [xn + xx * mu[i] for i in range(6)]
    w_in = W['a_w_in'][li]
    w_rkv = w_in[:, :3 * MIX_WIDTH].reshape(D, 3, MIX_WIDTH)
    rkv = jnp.einsum('sbtd,dsc->sbtc', jnp.stack([xr, xk, xv]), w_rkv)
    r, k, v = rkv[0], rkv[1], rkv[2]
    q_mem = xn @ w_in[:, 3 * MIX_WIDTH:]
    w_log = -jax.nn.softplus(-(W['a_w0'][li] + jnp.tanh(xw @ W['a_w1'][li]) @ W['a_w2'][li])) - 0.5
    decay = jnp.exp(-jnp.exp(w_log.astype(f32)))
    a = jax.nn.sigmoid(W['a_a0'][li] + (xa @ W['a_a1'][li]) @ W['a_a2'][li])
    if v_first is not None:
        vi = li - 1
        v = v + (v_first - v) * jax.nn.sigmoid(W['a_v0'][vi] + (xv @ W['a_v1'][vi]) @ W['a_v2'][vi])
    g = jax.nn.sigmoid(xg @ W['a_g1'][li]) @ W['a_g2'][li]
    heads = lambda t: t.astype(f32).reshape(B, T, RWKV_HEADS, HEAD_DIM)
    kk = heads(k * W['a_k_k'][li])
    kk = kk / jnp.maximum(jnp.sqrt(jnp.sum(kk * kk, axis=-1, keepdims=True)), 1e-12)
    k = k * (1.0 + (a - 1.0) * W['a_k_a'][li])
    rh, kh, vh, ah, wh = heads(r), heads(k), heads(v), heads(a), heads(decay)
    S, o = wkv7_scan(S0.astype(f32), rh, wh, kh, vh, kk, ah)
    mean = jnp.mean(o, axis=-1, keepdims=True)
    var = jnp.mean(jnp.square(o - mean), axis=-1, keepdims=True)
    o = ((o - mean) * lax.rsqrt(var + LNX_EPS)).reshape(B, T, MIX_WIDTH)
    o = o * W['a_lnx_w'][li].astype(f32) + W['a_lnx_b'][li].astype(f32)
    bonus = jnp.sum(rh * kh * W['a_r_k'][li].astype(f32), axis=-1, keepdims=True) * vh
    o = (o + bonus.reshape(B, T, MIX_WIDTH)) * g.astype(f32)
    return o.astype(xn.dtype), q_mem, S, v

def shared_kv(h, pos, g_kv, w_kv):
    B, T, _ = h.shape
    kv = (rms_norm(h, g_kv) @ w_kv).reshape(B, T, 2, N_GROUPS, GROUP_HEADS, HEAD_DIM)
    return rotary(kv[:, :, 0], pos), kv[:, :, 1]

def prompt_sources(k_sh, v_sh):
    T = k_sh.shape[1]
    srcs, bufs = [], []
    for g, (win, _) in enumerate(DIL_GROUPS):
        kg, vg = k_sh[:, :, g], v_sh[:, :, g]
        srcs.append((kg, vg, 0))
        L = min(win, PAST_LEN)
        kv = jnp.stack([kg, vg], axis=2)
        if T < L:
            kv = jnp.pad(kv, ((0, 0), (L - T, 0), (0, 0), (0, 0), (0, 0)))
        bufs.append(kv[:, -L:])
    return srcs, bufs

def sample_sources(k_sh, v_sh, win_bufs):
    srcs, bufs = [], []
    for g, buf in enumerate(win_bufs):
        L = buf.shape[1]
        ks = jnp.concatenate([buf[:, :, 0].astype(k_sh.dtype), k_sh[:, :, g]], axis=1)
        vs = jnp.concatenate([buf[:, :, 1].astype(v_sh.dtype), v_sh[:, :, g]], axis=1)
        srcs.append((ks, vs, L))
        bufs.append(jnp.stack([ks, vs], axis=2)[:, -L:])
    return srcs, bufs

def dilated_group_attn(q, ks, vs, idx, valid):
    kg = ks[:, idx]
    vg = vs[:, idx]
    s = jnp.einsum('bqhd,bqjhd->bqhj', q, kg).astype(jnp.float32) * (HEAD_DIM ** -0.5)
    s = jnp.where(valid[None, :, None, :], s, -jnp.inf)
    lse = jax.nn.logsumexp(s, axis=-1)
    p = jnp.exp(s - lse[..., None]).astype(vs.dtype)
    return jnp.einsum('bqhj,bqjhd->bqhd', p, vg), lse

def dilated_attention(q, srcs):
    B, T = q.shape[:2]
    qb = Q_BLOCK if T % Q_BLOCK == 0 else T

    def block(bi):
        t0 = bi * qb
        tq = t0 + jnp.arange(qb)
        q_blk = lax.dynamic_slice_in_dim(q, t0, qb, axis=1)
        outs, lses = [], []
        for g, ((win, dil), (ks, vs, base)) in enumerate(zip(DIL_GROUPS, srcs)):
            offs = dil * jnp.arange(win // dil + 1)
            idx = base + tq[:, None] - offs[None, :]
            o, l = dilated_group_attn(q_blk[:, :, g], ks, vs, jnp.maximum(idx, 0), idx >= 0)
            outs.append(o)
            lses.append(l)
        alpha = jax.nn.softmax(jnp.stack(lses, axis=0), axis=0)
        o = jnp.sum(alpha[..., None] * jnp.stack(outs, axis=0).astype(jnp.float32), axis=0)
        return o.astype(q.dtype)

    o = lax.map(block, jnp.arange(T // qb))
    return jnp.moveaxis(o, 0, 1).reshape(B, T, GROUP_HEADS, HEAD_DIM)

def run_trunk(h, pos, mem_kv_all, wkv0, shift0, win_bufs, W):
    B, T, _ = h.shape
    new_wkv, new_shift, new_bufs = [], [], []
    v_first = None
    srcs = None
    for l in range(DEPTH):
        xn = rms_norm(h, W['g_pre_mix'][l])
        mk, mv = mem_kv_all[l][:, :, 0], mem_kv_all[l][:, :, 1]
        if l < N_A_LAYERS:
            o_mix, q_mem, S, v = rwkv7_layer(xn, shift0[l], wkv0[l], v_first, l, W)
            if l == 0:
                v_first = v
            new_wkv.append(S)
            new_shift.append(xn[:, -1])
            w_out = W['a_w_out'][l]
        else:
            if l == N_A_LAYERS:
                k_sh, v_sh = shared_kv(h, pos, W['g_kv'], W['w_kv'])
                if win_bufs is None:
                    srcs, new_bufs = prompt_sources(k_sh, v_sh)
                else:
                    srcs, new_bufs = sample_sources(k_sh, v_sh, win_bufs)
            j = l - N_A_LAYERS
            proj = xn @ W['b_w_in'][j]
            q = rotary(proj[..., :MIX_WIDTH].reshape(B, T, N_GROUPS, GROUP_HEADS, HEAD_DIM), pos)
            q_mem = proj[..., MIX_WIDTH:]
            o_mix = dilated_attention(q, srcs).reshape(B, T, DIL_WIDTH)
            w_out = W['b_w_out'][j]
        o_mem = mem_attention(q_mem.reshape(B, T, MEM_HEADS, HEAD_DIM), mk, mv).reshape(B, T, MEM_WIDTH)
        mixed = jnp.concatenate([o_mix.astype(h.dtype), o_mem.astype(h.dtype)], axis=-1) @ w_out
        h = h + rms_norm(mixed, W['g_post_mix'][l])
        f = rms_norm(h, W['g_pre_ffn'][l]) @ W['w_ffn_in'][l]
        f = (jax.nn.silu(f[..., :D_FF]) * f[..., D_FF:]) @ W['w_ffn_out'][l]
        h = h + rms_norm(f, W['g_post_ffn'][l])
    return h, jnp.stack(new_wkv), jnp.stack(new_shift), new_bufs

def setup_inputs(seed: int = 0) -> dict:
    key = jax.random.key(seed)
    keys = iter(jax.random.split(key, 64))

    def nrm(shape, scale):
        return scale * jax.random.normal(next(keys), shape, jnp.float32)

    def gain(shape):
        return 1.0 + nrm(shape, 0.05)

    D = D_MODEL
    L0, L1, L2 = [min(w, PAST_LEN) for w, _ in DIL_GROUPS]
    NA, NB = N_A_LAYERS, N_B_LAYERS
    return {
        'x_prompt': nrm((BATCH, SEQ, D), 1.0),
        'x_sample': nrm((DEC_BATCH, DEC_SEQ, D), 1.0),
        'state_wkv': nrm((NA, DEC_BATCH, RWKV_HEADS, HEAD_DIM, HEAD_DIM), 0.1),
        'state_shift': nrm((NA, DEC_BATCH, D), 1.0),
        'cache_win_g0': nrm((DEC_BATCH, L0, 2, GROUP_HEADS, HEAD_DIM), 1.0),
        'cache_win_g1': nrm((DEC_BATCH, L1, 2, GROUP_HEADS, HEAD_DIM), 1.0),
        'cache_win_g2': nrm((DEC_BATCH, L2, 2, GROUP_HEADS, HEAD_DIM), 1.0),
        'cache_mem': nrm((DEPTH, DEC_BATCH, MEM_TOKENS, 2, MEM_HEADS, HEAD_DIM), 1.0),
        'mem_prompt': nrm((BATCH, MEM_TOKENS, D), 1.0),
        'g_pre_mix': gain((DEPTH, D)),
        'g_post_mix': gain((DEPTH, D)),
        'g_pre_ffn': gain((DEPTH, D)),
        'g_post_ffn': gain((DEPTH, D)),
        'g_mem': gain((DEPTH, D)),
        'w_mem_kv': nrm((DEPTH, D, 2 * MEM_WIDTH), D ** -0.5),
        'w_ffn_in': nrm((DEPTH, D, 2 * D_FF), D ** -0.5),
        'w_ffn_out': nrm((DEPTH, D_FF, D), D_FF ** -0.5),
        'a_mu': 0.5 + nrm((NA, 6, D), 0.2),
        'a_w_in': nrm((NA, D, 3 * MIX_WIDTH + MEM_WIDTH), D ** -0.5),
        'a_w0': -1.0 + nrm((NA, MIX_WIDTH), 1.0),
        'a_w1': nrm((NA, D, LORA_W), D ** -0.5),
        'a_w2': nrm((NA, LORA_W, MIX_WIDTH), 0.1 * LORA_W ** -0.5),
        'a_a0': nrm((NA, MIX_WIDTH), 0.1),
        'a_a1': nrm((NA, D, LORA_A), D ** -0.5),
        'a_a2': nrm((NA, LORA_A, MIX_WIDTH), 0.1 * LORA_A ** -0.5),
        'a_v0': nrm((NA - 1, MIX_WIDTH), 0.1),
        'a_v1': nrm((NA - 1, D, LORA_V), D ** -0.5),
        'a_v2': nrm((NA - 1, LORA_V, MIX_WIDTH), 0.1 * LORA_V ** -0.5),
        'a_g1': nrm((NA, D, LORA_G), D ** -0.5),
        'a_g2': nrm((NA, LORA_G, MIX_WIDTH), LORA_G ** -0.5),
        'a_k_k': 0.85 + nrm((NA, MIX_WIDTH), 0.05),
        'a_k_a': 1.0 + nrm((NA, MIX_WIDTH), 0.05),
        'a_r_k': nrm((NA, RWKV_HEADS, HEAD_DIM), 0.1),
        'a_lnx_w': gain((NA, MIX_WIDTH)),
        'a_lnx_b': nrm((NA, MIX_WIDTH), 0.02),
        'a_w_out': nrm((NA, MIX_WIDTH + MEM_WIDTH, D), (MIX_WIDTH + MEM_WIDTH) ** -0.5),
        'g_kv': gain((D,)),
        'w_kv': nrm((D, 2 * MIX_WIDTH), D ** -0.5),
        'b_w_in': nrm((NB, D, MIX_WIDTH + MEM_WIDTH), D ** -0.5),
        'b_w_out': nrm((NB, DIL_WIDTH + MEM_WIDTH, D), (DIL_WIDTH + MEM_WIDTH) ** -0.5),
    }

def reference(x_prompt, x_sample, state_wkv, state_shift, cache_win_g0, cache_win_g1, cache_win_g2,
              cache_mem, mem_prompt, g_pre_mix, g_post_mix, g_pre_ffn, g_post_ffn, g_mem, w_mem_kv,
              w_ffn_in, w_ffn_out, a_mu, a_w_in, a_w0, a_w1, a_w2, a_a0, a_a1, a_a2, a_v0, a_v1, a_v2,
              a_g1, a_g2, a_k_k, a_k_a, a_r_k, a_lnx_w, a_lnx_b, a_w_out, g_kv, w_kv, b_w_in, b_w_out):
    W = dict(g_pre_mix=g_pre_mix, g_post_mix=g_post_mix, g_pre_ffn=g_pre_ffn, g_post_ffn=g_post_ffn,
             w_ffn_in=w_ffn_in, w_ffn_out=w_ffn_out, a_mu=a_mu, a_w_in=a_w_in, a_w0=a_w0, a_w1=a_w1,
             a_w2=a_w2, a_a0=a_a0, a_a1=a_a1, a_a2=a_a2, a_v0=a_v0, a_v1=a_v1, a_v2=a_v2, a_g1=a_g1,
             a_g2=a_g2, a_k_k=a_k_k, a_k_a=a_k_a, a_r_k=a_r_k, a_lnx_w=a_lnx_w, a_lnx_b=a_lnx_b,
             a_w_out=a_w_out, g_kv=g_kv, w_kv=w_kv, b_w_in=b_w_in, b_w_out=b_w_out)
    Bp, Tp, _ = x_prompt.shape
    Ts = x_sample.shape[1]
    mem_kv_p = jnp.stack([mem_kv(mem_prompt, g_mem[l], w_mem_kv[l]) for l in range(DEPTH)])
    wkv_zero = jnp.zeros((N_A_LAYERS, Bp, RWKV_HEADS, HEAD_DIM, HEAD_DIM), jnp.float32)
    shift_zero = jnp.zeros((N_A_LAYERS, Bp, D_MODEL), x_prompt.dtype)
    pos_p = jnp.arange(Tp, dtype=jnp.int32)
    y_p, wkv_p, shift_p, bufs_p = run_trunk(x_prompt, pos_p, mem_kv_p, wkv_zero, shift_zero, None, W)
    pos_s = PAST_LEN + jnp.arange(Ts, dtype=jnp.int32)
    y_s, wkv_s, shift_s, bufs_s = run_trunk(x_sample, pos_s, cache_mem, state_wkv, state_shift,
                                            [cache_win_g0, cache_win_g1, cache_win_g2], W)
    return (y_p, y_s, wkv_p, shift_p, bufs_p[0], bufs_p[1], bufs_p[2], mem_kv_p,
            wkv_s, shift_s, bufs_s[0], bufs_s[1], bufs_s[2])


_drawn_inputs = setup_inputs


def setup_inputs(seed=0):
    import zlib

    import numpy as np

    out = dict(_drawn_inputs(seed))
    spreads = {}
    factors = {'a_w1': 4.887, 'a_w2': 5.03, 'a_k_k': 2.815}
    for name, (base, spread) in spreads.items():
        noise = np.random.default_rng([zlib.crc32(name.encode()), seed]).standard_normal(out[name].shape)
        drawn = base * np.exp(spread * noise) if base else spread * noise
        out[name] = __import__('jax').numpy.asarray(drawn.astype(out[name].dtype))
    for name, factor in factors.items():
        out[name] = (out[name] * factor).astype(out[name].dtype)
    return out
```

```python
from contextlib import ExitStack

import concourse.bass as bass
from concourse import mybir

ALU = mybir.AluOpType
ACT = mybir.ActivationFunctionType
F32 = mybir.dt.float32
AX_X = mybir.AxisListType.X

P = 128
D = 1024
KD = D // P
TP, NB, TS = 512, 8, 8
NS = NB * TS
T = TP + NS
HALF = T // 2
HD = 64
MIX = 3 * D // 4
CM = MIX // P
FF = 2816
KF = FF // P
C = 64
NCH = T // C
SAMPLE = NCH - 1
LEVELS = 6
SAMPLE_LEVELS = 3
MEMT = 256
SCALE = HD ** -0.5
NEG = -1e30

MU, G_PRE, G_POST, G_PRE_F, G_POST_F, G_MEM, G_KV, SHIFT = 0, 6, 8, 10, 12, 14, 16, 17
W0, A0, K_K, K_A, R_K, LNX_W, LNX_B = 25, 26, 27, 28, 29, 30, 31
NVEC, NVEC_D = 32, 25

CONSTS, _at = {}, 0
for _n, _w in (("ident", 128), ("mean", 128), ("pair", 128), ("swap", 128), ("carry", T),
               ("before", C), ("upto", C), ("before_s", C), ("upto_s", C), ("level", LEVELS * C),
               ("ids", C), ("in_batch", NB * C), ("of_batch", NB), ("eps", 1), ("lnx_eps", 1),
               ("ln_shift", 1)):
    CONSTS[_n] = (_at, _at + _w)
    _at += _w
NCONST = _at
KEYS_S = 512 + 512 + 128 + 3 * NS
KEYS_P = TP + 2 * P


SLOT = CM * T
A_R, A_K, A_V, A_A, A_LW, A_KK, A_BON, A_CL, A_TMP, A_G = [i * SLOT for i in range(10)]
A_WK = 10 * SLOT
BIG = KD * T
A_XN, A_XD, A_X1, A_X2 = A_KK, A_KK + BIG, A_KK + 2 * BIG, A_G
A_H0 = A_G
A_CAT = A_K
A_H = A_KK
A_SQ = A_H + BIG
A_Y = A_SQ + BIG
A_XF = A_G
A_F = 0
A_U = KF * T
A_RSTD = A_WK + 2688
PROBS = 1344
PT = 11 * P
ATT = ({"cat": A_CAT, "p": 8064, "pt": 10752, "qs": 13568, "kt": 14080, "k": 15104, "v": 15104},
       {"cat": 18432, "p": 20736, "pt": 5504, "qs": 3456, "kt": 24832, "v": 29440, "k": 34048})
PT1_L1 = 23424
A_QC, A_KC, A_VC, A_ROTQ, A_ROTK, A_COS, A_KVT = 6912, 0, 3456, 10368, A_G, 13824, 21888
A_MASKP, A_MASKS, A_VCLASS, A_V0, A_VS = 10368, 12672, 14592, 16640, 17664
A_YT = 0
ARENA = A_WK + 3840
WCOL = 2816
RING = 3


def trunk(nc, I, O):

    units = []
    tiles = 0

    def rows(w):
        return w.rearrange("(k p) n -> p k n", p=P)

    def add(src, nk, n, done, parts=P):
        nonlocal tiles
        tiles += done
        units.append((src, nk, n, tiles, parts))

    def add_cols(w, c0, n, nk, step=256):
        for c in range(c0, c0 + n, step):
            add(rows(w)[:, :, c:c + step], nk, step, step // P)

    for l in range(2):
        add_cols(I["w_mem_kv"][l], 0, 512, KD)
    L0 = tiles
    w_in = I["a_w_in"][0]
    add_cols(w_in, 3 * MIX, 256, KD)
    add_cols(w_in, 0, MIX, KD)
    END_R = tiles
    add(rows(I["a_w1"][0]), KD, 64, 1)
    END_W1 = tiles
    add(I["a_w2"][0].unsqueeze(1), 1, MIX, CM, 64)
    add_cols(w_in, MIX, MIX, KD)
    END_K = tiles
    add_cols(w_in, 2 * MIX, MIX, KD)
    END_V = tiles
    add(rows(I["a_a1"][0]), KD, 64, 1)
    add(I["a_a2"][0].unsqueeze(1), 1, MIX, CM, 64)
    add(rows(I["a_g1"][0]), KD, 128, 1)
    add(I["a_g2"][0].unsqueeze(1), 1, MIX, CM)
    END_PROJ = tiles
    SUMS = 2 * CM
    tiles += SUMS
    add_cols(I["a_w_out"][0], 0, D, KD)
    END_OUT0 = tiles

    def add_ffn(l):
        for u in range(FF // 256):
            add_cols(I["w_ffn_in"][l], u * 256, 256, KD)
            add_cols(I["w_ffn_in"][l], FF + u * 256, 256, KD)
        add_cols(I["w_ffn_out"][l], 0, D, KF, P)

    add_ffn(0)
    END_F0 = tiles
    add_cols(I["w_kv"], 0, 2 * MIX, KD)
    add_cols(I["b_w_in"][0], 0, D, KD)
    END_QKV = tiles
    ROT = 2 * CM
    tiles += ROT
    add_cols(I["b_w_out"][0], 0, D, 4)
    END_OUT1 = tiles
    add_ffn(1)
    END_F1 = tiles

    with ExitStack() as ctx:
        def sb(name, shape):
            return ctx.enter_context(nc.sbuf_tensor(name, shape, F32))

        def sem(name):
            return ctx.enter_context(nc.semaphore(name))

        banks = ctx.enter_context(nc.psum_tensor("banks", [P, 8, 512], F32))
        arena = sb("arena", [P, ARENA])
        ring = sb("ring", [P, RING, WCOL])
        consts = sb("consts", [P, NCONST])
        vec = sb("vec", [P, KD, NVEC])
        mkv = sb("mkv", [P, 2, 512])
        mkt = sb("mkt", [P, 2, MEMT])
        qmem = sb("qmem", [P, 2, T])
        decay_end = sb("decay_end", [P, CM, 16])
        state = sb("state", [P, 2, CM, HD])
        small = sb("small", [P, 64])

        h_scratch = nc.dram_tensor("h_scratch", [P, BIG], F32).ap()
        mkv_scratch = nc.dram_tensor("mkv_scratch", [P, 2 * 512], F32).ap()

        def const(name):
            a, b = CONSTS[name]
            return consts[:, a:b]

        def at(off, *dims, parts=P):
            n = 1
            for d in dims:
                n *= d
            v = arena[0:parts, off:off + n]
            names = [f"d{i}" for i in range(len(dims))]
            if len(dims) == 1:
                return v
            sizes = {k: d for k, d in zip(names, dims)}
            return v.rearrange(f"p ({' '.join(names)}) -> p {' '.join(names)}", **sizes)

        ident = const("ident")
        o_centred = consts[:, CONSTS["carry"][0]:CONSTS["carry"][0] + CM * C].rearrange("p (c v) -> p c v", c=CM)

        xtok = at(0, 4, D)
        xs_tok = at(4096, D, parts=NS)
        mem_tok = at(5120, 2, D)
        mem_t = at(7168, KD, MEMT)
        mem_g = at(9216, 2, KD, MEMT)
        vrows = at(13312, D, parts=NVEC)
        mkv1 = at(14336, 2, 512)
        shift_out = at(15360, D, parts=9)
        xlast = at(16384, KD, 9)
        assert 16384 + 72 <= A_KK
        h0 = at(A_H0, KD, T)

        xn = at(A_XN, KD, T)
        xd = at(A_XD, KD, T)
        xmix = [at(A_X1, KD, T), at(A_X2, KD, T)]
        sq0 = at(A_XD, KD, T)
        lora_mid = [arena[:, A_WK + 1152 + i * T:A_WK + 1152 + (i + 1) * T] for i in range(3)]
        ln_ms = arena[:, A_RSTD:A_RSTD + T]
        rstd = arena[:, A_RSTD + T:A_RSTD + 2 * T]
        R, K, V, A, LW, KK, BON, CL, TMP, G = [at(i * SLOT, CM, T) for i in range(10)]

        h = at(A_H, KD, T)
        sq = at(A_SQ, KD, T)
        y = at(A_Y, KD, T)
        cat = at(A_CAT, KD, T)
        xf = at(A_XF, KD, T)
        ff = at(A_F, KF, T)
        up = at(A_U, 2, T)

        def flat(v):
            return v.rearrange("p a b -> p (a b)")

        zero_rows = at(16640, 512)
        def wk(i, off=A_WK):
            return at(off + i * CM * C, CM, C)

        xt_all = [at(A_LW + j * CM * C, CM, C) for j in range(NCH)]
        inv_bufs = [[wk(4 * i + n) for n in range(4)] for i in range(2)]
        prep = [[wk(n) for n in range(6)], [wk(n, A_CL) for n in range(6)]]
        u_buf, sa_buf = wk(6), wk(7)
        s0t = at(A_CL, CM, NB, HD)
        masked = at(A_CL + CM * NB * HD, CM, NB, HD)
        s0_raw = at(A_CL + CM * NB * HD, NB, CM, HD)
        o_buf = [wk(8), at(A_CL + 2 * CM * NB * HD, CM, C)]
        on_buf = [wk(9), at(A_CL + 2 * CM * NB * HD + CM * C, CM, C)]
        order = [SAMPLE] + list(range(SAMPLE))
        groups = [(0, 1), (2, 3), (4, 5), (6, 7), (SAMPLE,)]

        def levels(j):
            return SAMPLE_LEVELS if j == SAMPLE else LEVELS

        def cols(j):
            return slice(j * C, (j + 1) * C)

        def hp(i):
            return slice(HD * i, HD * i + HD)

        def over(v, n):
            return v.unsqueeze(1).broadcast_to([v.shape[0], n, v.shape[1]])

        def each(v, n):
            return v.unsqueeze(2).broadcast_to([v.shape[0], v.shape[1], n])

        def bankpair(n, m=P):
            s = n % 3
            return banks[0:m, 2 * s:2 * s + 2, 0:HALF]

        def halves(v):
            return v.rearrange("p (a b) -> p a b", a=2)

        PAIRS = NB // 2
        steps = [[("mem_p", t, hd) for t in range(4) for hd in range(4)] + [("mem_s", g, 0) for g in range(PAIRS)],
                 [("mem_p", t, hd) for t in range(4) for hd in range(4)] + [("mem_s", g, 0) for g in range(PAIRS)]
                 + [("dil_p", r, hd) for r in range(4) for hd in range(4)] + [("dil_s", g, 0) for g in range(PAIRS)]]
        ROWS = {"mem_p": P, "mem_s": 64, "dil_p": P, "dil_s": 64}
        WIDTH = {"mem_p": MEMT, "mem_s": MEMT, "dil_p": KEYS_P, "dil_s": KEYS_S}
        TURNS = {"mem_p": [[(0, 128), (128, 128)]], "mem_s": [[(0, 128), (128, 128)]],
                 "dil_p": [[(i * P, P) for i in range(4)], [(512, P), (640, P)]],
                 "dil_s": [[(i * P, P) for i in range(8)], [(1024, P), (1152, NS), (1216, NS), (1280, NS)]]}
        att = [{}, {}]
        for l in range(2):
            a, o = att[l], ATT[l]
            a["cat"] = at(o["cat"], KD if l == 0 else 4, T)
            a["mem_tile"] = CM if l == 0 else 2
            a["p"] = [at(o["p"] + i * PROBS, PROBS) for i in range(2)]
            a["pt"] = [at(o["pt"], PT), at(o["pt"] + PT if l == 0 else PT1_L1, PT)]
            a["qs"] = [at(o["qs"] + i * 512, NB, 2, 4 * TS) for i in range(1 if l == 0 else 4)]
            a["kt"] = [at(o["kt"] + i * 512, 2, MEMT) for i in range(2)]
            a["kv"] = [at(o["v"] + i * 1024, 2, 512) for i in range(2)]
        kc, qc, vc = at(A_KC, CM, T), at(A_QC, CM, T), at(A_VC, CM, T)
        rot = [at(A_ROTQ, CM, T), at(A_ROTK, CM, T)]
        cos_sin = at(A_COS, 2, T)
        kv_tok = at(A_KVT, 4, 2, MIX)
        kv_new = at(A_KVT + 4 * 2 * MIX, 2, MIX, parts=NS)
        mask_p = at(A_MASKP, 4 * TP + 2 * P)
        mask_s = at(A_MASKS, 1152 + PAIRS * 3 * NS, parts=64)
        v_class = at(A_VCLASS, 4, 2, 256)
        v_tok = at(A_V0, 4, 256)
        v_new = at(A_VS, 3, 256, parts=NS)
        kt_dil = [at(ATT[1]["kt"] + i * 2304, 2304) for i in range(2)]
        v_dil = [at(ATT[1]["v"] + i * 2304, 9, 256) for i in range(2)]
        k_dil = at(ATT[1]["k"], 9, 256)
        KT1, KT2, KT0 = 0, 1024, 2048
        xkv = at(A_Y, KD, T)
        y_tok = at(A_YT, 4, D)
        y_new = at(A_YT + 4 * D, D, parts=NS)
        ATT_KEYS = {0: 1, 1: 3}

        def turn_order(l):
            out, todo = [], []
            for n, (kind, x, _) in enumerate(steps[l]):
                if kind in ("mem_s", "dil_s") and x:
                    out += [("end", m) for m in todo]
                    todo = []
                out.append(("begin", n))
                out += [("end", m) for m in todo]
                todo = [n]
            return out + [("end", m) for m in todo]

        KEY_TURNS = {"mem_s": 1, "dil_s": 5}

        def turns_before(l, kind, batch):
            n = 0
            for what, m in turn_order(l):
                k, x, _ = steps[l][m]
                if what == "end":
                    n += len(TURNS[k])
                    continue
                for b in range(2) if k in KEY_TURNS else ():
                    n += KEY_TURNS[k]
                    if batch is not None and (k, 2 * x + b) == (kind, batch):
                        return n
            return n

        NT0 = turns_before(0, None, None)
        NTA = NT0 + 15 + 4
        NT1 = NTA + turns_before(1, None, None)
        KV_STORES = 2 * (1 + 8 + 3 * NB)

        def banks3(q):
            s = 3 * (q % 2)
            return banks[:, s:s + 3, :].rearrange("p a b -> p (a b)")

        zeroed = sem("zeroed")
        consts_in, vrows_in, x_in, xs_in, mem_in = [sem(n) for n in (
            "consts_in", "vrows_in", "x_in", "xs_in", "mem_in")]
        weights_in = [sem(f"weights_in{i}") for i in range(RING)]
        tile_ready, tile_free = sem("tile_ready"), sem("tile_free")
        vec_t, vec_ready = sem("vec_t"), sem("vec_ready")
        xt_ready, xt_free = sem("xt_ready"), sem("xt_free")
        mem_scaled, mt_ready, mt_free, mem_g_ready = [sem(n) for n in (
            "mem_scaled", "mt_ready", "mt_free", "mem_g_ready")]
        sq_ready, ms_ready, rstd_ready = [sem(n) for n in ("sq_ready", "ms_ready", "rstd_ready")]
        xn_ready, xlast_ready, xlast_t, shift_ready = [sem(n) for n in (
            "xn_ready", "xlast_ready", "xlast_t", "shift_ready")]
        mix_ready = sem("mix_ready")
        vchain, achain = sem("vector_chain"), sem("scalar_chain")
        h_ready, h_saved, h_back = sem("h_ready"), sem("h_saved"), sem("h_back")
        kv_saved, kv_back, phase_a_stored = sem("kv_saved"), sem("kv_back"), sem("phase_a_stored")
        out_done = sem("out_done")
        mkt_t, mkt_ready = sem("mkt_t"), sem("mkt_ready")
        cat_ready = sem("cat_ready")
        u_ready, f_ready = sem("u_ready"), sem("f_ready")
        kk_ready, kk_sq, ss_clamped, kk_scale, rk_ready = [sem(n) for n in (
            "kk_ready", "kk_sq", "ss_clamped", "kk_scale", "rk_ready")]
        cum_ready, grown, shrunk, factors_ready = [sem(n) for n in (
            "cum_ready", "grown", "shrunk", "factors_ready")]
        grown_used, shifted = sem("grown_used"), sem("shifted")
        inv_l, inv_lsb, inv_y, inv_ysb, inv_d, inv_x = [sem(n) for n in (
            "inv_l", "inv_lsb", "inv_y", "inv_ysb", "inv_d", "inv_x")]
        s0_in, s0_t, s0_ready = sem("s0_in"), sem("s0_t"), sem("s0_ready")
        masked_ready = sem("masked_ready")
        turned, turned_out = sem("turned"), sem("turned_out")
        intra, intra_out = sem("intra"), sem("intra_out")
        u_psum, u_sb, sa_psum, sa_sb, o_psum, o_sb, ds_psum, s_new, on_ready = [sem(n) for n in (
            "u_psum", "u_sb", "sa_psum", "sa_sb", "o_psum", "o_sb", "ds_psum", "s_new", "on_ready")]
        dsm_psum, dsm_free, s0_scaled = sem("dsm_psum"), sem("dsm_free"), sem("s0_scaled")
        var_ready, gn_ready = sem("var_ready"), sem("gn_ready")
        st_t, st_out = sem("st_t"), sem("st_out")
        sm_s, sm_max, sm_exp, sm_p, sm_t, sm_pt, sm_o, sm_cat = [sem(n) for n in (
            "sm_s", "sm_max", "sm_exp", "sm_p", "sm_t", "sm_pt", "sm_o", "sm_cat")]
        qs_ready = sem("qs_ready")
        keys_in, vals_in = sem("keys_in"), sem("vals_in")
        cos_in, masks_in, rotated, kv_turned, v_copied, y_turned = [sem(n) for n in (
            "cos_in", "masks_in", "rotated", "kv_turned", "v_copied", "y_turned")]
        kv_stored = sem("kv_stored")

        block = ctx.enter_context(nc.Block())

        @block.sync
        def _(sp):
            sp.dma_start(consts[:, :], I["consts"]).then_inc(consts_in, 16)
            for src, r, n in ((I["a_mu"][0], MU, 6), (I["g_pre_mix"], G_PRE, 2), (I["g_post_mix"], G_POST, 2),
                              (I["g_pre_ffn"], G_PRE_F, 2), (I["g_post_ffn"], G_POST_F, 2), (I["g_mem"], G_MEM, 2),
                              (I["g_kv"].unsqueeze(0), G_KV, 1), (I["state_shift"][0], SHIFT, NB)):
                sp.dma_start(vrows[r:r + n, :], src).then_inc(vrows_in, 16)
            for src, r in ((I["a_w0"], W0), (I["a_a0"], A0), (I["a_k_k"], K_K), (I["a_k_a"], K_A),
                           (I["a_r_k"].rearrange("a h d -> a (h d)"), R_K), (I["a_lnx_w"], LNX_W),
                           (I["a_lnx_b"], LNX_B)):
                sp.dma_start(vrows[r:r + 1, 0:MIX], src).then_inc(vrows_in, 16)
            sp.dma_start(mem_tok, I["mem_prompt"][0].rearrange("(m p) d -> p m d", p=P)).then_inc(mem_in, 16)
            sp.dma_start(xtok, I["x_prompt"][0].rearrange("(m p) d -> p m d", p=P)).then_inc(x_in, 16)
            sp.dma_start(xs_tok, I["x_sample"].rearrange("b t d -> (b t) d")).then_inc(xs_in, 16)
            for n, (src, nk, w, _, parts) in enumerate(units):
                if n >= RING:
                    sp.wait_ge(tile_ready, units[n - RING][3])
                dst = ring[0:parts, n % RING, 0:nk * w].rearrange("p (k n) -> p k n", k=nk)
                sp.dma_start(dst, src).then_inc(weights_in[n % RING], 16)

        @block.gpsimd
        def _(pool):
            stores = [0]

            def store(dst, src):
                stores[0] += 1
                pool.dma_start(dst, src).then_inc(out_done, 16)

            nc.gpsimd.memset(zero_rows, 0.0).then_inc(zeroed, 1)
            pool.wait_ge(zeroed, 1)
            pool.dma_start(O[6][0, 0:TP].rearrange("(p r) k h d -> p (r k h d)", p=P).rearrange("p (n z) -> p n z", z=512),
                           over(zero_rows, 4)).then_inc(phase_a_stored, 16)
            pool.wait_ge(xt_free, KD + 1)
            pool.dma_start(h_scratch, flat(h0)).then_inc(h_saved, 16)
            pool.wait_ge(tile_free, 4)
            store(O[7][0, 0].rearrange("(m p) k h d -> p m (k h d)", p=P), mkv[:, :, :])
            pool.wait_ge(tile_free, 8)
            pool.dma_start(O[7][1, 0].rearrange("(m p) k h d -> p m (k h d)", p=P), mkv1).then_inc(phase_a_stored, 16)
            pool.dma_start(mkv_scratch, flat(mkv1)).then_inc(phase_a_stored, 16)
            for name, o in (("cache_win_g0", 10), ("cache_win_g1", 11), ("cache_win_g2", 12)):
                L = I[name].shape[1]
                store(O[o][:, 0:L - TS].rearrange("b l k h d -> b (l k h d)"),
                      I[name][:, TS:L].rearrange("b l k h d -> b (l k h d)"))
            pool.wait_ge(shift_ready, 1)
            pool.dma_start(O[3][0], shift_out[0:1, :]).then_inc(phase_a_stored, 16)
            pool.dma_start(O[9][0], shift_out[1:9, :]).then_inc(phase_a_stored, 16)
            pool.wait_ge(factors_ready, 1)
            for c in range(CM):
                pool.dma_start(s0_raw[:, :, c, :], I["state_wkv"][0].rearrange("b (c h) v k -> (h v) b c k", h=2)[:, :, c, :]).then_inc(s0_in, 16)
            pool.wait_ge(st_out, CM)
            for c in range(CM):
                store(O[8][0].rearrange("b (c h) v k -> (h v) b c k", h=2)[:, :, c, :], s0_raw[:, :, c, :])
            pool.wait_ge(st_out, CM + 1)
            store(O[2][0, 0].rearrange("(c h) v k -> (h v) c k", h=2), prep[0][0])
            pool.wait_ge(cat_ready, 1)
            pool.wait_ge(h_saved, 16)
            pool.dma_start(flat(h), h_scratch).then_inc(h_back, 16)

            def memory_rows(l):
                first = 0 if l == 0 else len(steps[0])
                for g in range(PAIRS):
                    q = first + 16 + g
                    if g:
                        pool.wait_ge(sm_o, q)
                    for i in range(2):
                        pool.dma_start(att[l]["kv"][i],
                                       I["cache_mem"][l, 2 * g + i].rearrange("(m p) k h d -> p m (k h d)", p=P)).then_inc(vals_in, 16)

            memory_rows(0)
            pool.wait_ge(rstd_ready, 4)
            pool.wait_ge(sm_cat, len(steps[0]))
            pool.wait_ge(phase_a_stored, 16 * 5)
            pool.dma_start(flat(mkv[:, :, :]), mkv_scratch).then_inc(kv_back, 16)
            pool.wait_ge(h_ready, 2)
            pool.dma_start(h_scratch, flat(h)).then_inc(h_saved, 16)
            pool.dma_start(cos_sin, I["cos_sin"]).then_inc(cos_in, 16)
            pool.wait_ge(sm_pt, NT0 + 15)
            kv_view = lambda o, a, b: O[o][0, a:b].rearrange("(m p) k h d -> p m k (h d)", p=P)

            def store_kv(dst, src):
                pool.dma_start(dst, src).then_inc(kv_stored, 16)

            for k in range(2):
                store_kv(kv_view(4, 0, P)[:, 0, k], kv_tok[:, 3, k, 0:256])
                for m in range(4):
                    store_kv(kv_view(5, 0, TP)[:, m, k], kv_tok[:, m, k, 256:512])
                    store_kv(kv_view(6, TP, 2 * TP)[:, m, k], kv_tok[:, m, k, 512:768])
                for g in range(3):
                    L = I[f"cache_win_g{g}"].shape[1]
                    for b in range(NB):
                        store_kv(O[10 + g][b, L - TS:L, k].rearrange("t h d -> t (h d)"),
                                 kv_new[b * TS:(b + 1) * TS, k, g * 256:(g + 1) * 256])
            pool.wait_ge(rotated, 2)
            pool.dma_start(mask_p, I["mask_p"]).then_inc(masks_in, 16)
            pool.dma_start(mask_s, I["mask_s"]).then_inc(masks_in, 16)
            pool.wait_ge(v_copied, 1)
            pool.wait_ge(kv_stored, KV_STORES * 16)
            memory_rows(1)
            n0 = len(steps[0]) + 36
            for g in range(PAIRS):
                pool.wait_ge(sm_o, n0 + g - (16 if g == 0 else 0))
                for i in range(2):
                    b = 2 * g + i
                    if b:
                        pool.wait_ge(sm_t, NTA + turns_before(1, "dil_s", b - 1))
                    for kv, dst, s in ((0, k_dil, keys_in), (1, v_dil[i], vals_in)):
                        pool.dma_start(dst[:, 0:4, :], I["cache_win_g1"][b, :, kv].rearrange("(m p) h d -> p m (h d)", p=P)).then_inc(s, 16)
                        for m in range(4):
                            rows16 = I["cache_win_g2"][b, m * 256:(m + 1) * 256, kv].rearrange("(j r) h d -> j r (h d)", r=16)
                            pool.dma_start(dst[:, 4 + m, :], rows16[:, 0:TS, :]).then_inc(s, 16)
                        pool.dma_start(dst[:, 8, :], I["cache_win_g0"][b, :, kv].rearrange("p h d -> p (h d)")).then_inc(s, 16)
            pool.wait_ge(tile_ready, END_OUT1)
            pool.wait_ge(h_saved, 32)
            pool.dma_start(flat(h), h_scratch).then_inc(h_back, 16)
            pool.wait_ge(sm_pt, NT1 + 8)
            store(O[0][0].rearrange("(m p) d -> p m d", p=P), y_tok)
            pool.wait_ge(sm_pt, NT1 + 10)
            store(O[1].rearrange("b t d -> (b t) d"), y_new)
            pool.wait_ge(out_done, 16 * stores[0])

        @block.tensor
        def _(pe):
            mm = nc.tensor.matmul
            tile = [0]
            unit = [0]

            def take():
                n = unit[0]
                unit[0] += 1
                _, nk, w, _, parts = units[n]
                pe.wait_ge(weights_in[n % RING], 16 * (n // RING + 1))
                return ring[0:parts, n % RING, 0:nk * w].rearrange("p (k n) -> p k n", k=nk)

            def next_tile():
                n = tile[0]
                tile[0] += 1
                if n >= 3:
                    pe.wait_ge(tile_free, n - 2)
                return 2 * (n % 3)

            def project(w, c0, m, x, nk, parts=P):
                s = next_tile()
                for k in range(nk):
                    for a in range(2):
                        last = mm(banks[0:m, s + a, 0:HALF], w[0:parts, k, c0:c0 + m],
                                  x[0:parts, k, a * HALF:(a + 1) * HALF], start=(k == 0), stop=(k == nk - 1))
                last.then_inc(tile_ready, 1)

            def project_cols(x, n, nk, step=256):
                for _ in range(n // step):
                    w = take()
                    for c in range(0, step, P):
                        project(w, c, P, x, nk)

            def mean_square(n, src):
                pe.wait_ge(sq_ready, n + 1)
                for k in range(KD):
                    for a in range(2):
                        last = mm(banks[:, 6 + a, 0:HALF], const("mean"), src[:, k, a * HALF:(a + 1) * HALF],
                                  start=(k == 0), stop=(k == KD - 1))
                last.then_inc(ms_ready, 1)

            pe.wait_ge(consts_in, 16)
            pe.wait_ge(vrows_in, 16 * 15)
            for k in range(KD):
                n = NVEC if k < CM else NVEC_D
                last = nc.tensor.transpose(banks[:, 6, k * NVEC:k * NVEC + n], vrows[0:n, k * P:(k + 1) * P], ident[0:n, 0:n])
            last.then_inc(vec_t, 1)
            for q in range(4):
                pe.wait_ge(mem_scaled, 2)
                for k in range(2 * q, 2 * q + 2):
                    for m in range(2):
                        last = nc.tensor.transpose(banks[:, q, (k % 2) * 256 + m * P:(k % 2) * 256 + (m + 1) * P],
                                                   mem_tok[:, m, k * P:(k + 1) * P], ident)
                last.then_inc(mt_ready, 1)
            pe.wait_ge(x_in, 16)
            for k in range(KD):
                if k >= 2:
                    pe.wait_ge(xt_free, k - 1)
                for m in range(4):
                    last = nc.tensor.transpose(banks[:, 4 + k % 2, m * P:(m + 1) * P], xtok[:, m, k * P:(k + 1) * P], ident)
                last.then_inc(xt_ready, 1)
            pe.wait_ge(xs_in, 16)
            for k in range(KD):
                last = nc.tensor.transpose(banks[:, 7, k * NS:(k + 1) * NS], xs_tok[:, k * P:(k + 1) * P], ident[0:NS, 0:NS])
            last.then_inc(xt_ready, 1)
            pe.wait_ge(mt_free, 4)
            pe.wait_ge(xt_free, KD)
            for l in range(2):
                pe.wait_ge(mem_g_ready, l + 1)
                for u in range(2):
                    w = take()
                    for m in range(2):
                        s = next_tile()
                        for k in range(KD):
                            last = mm(banks[:, s, 0:256], mem_g[:, l, k, m * P:(m + 1) * P], w[:, k, :],
                                      start=(k == 0), stop=(k == KD - 1))
                        last.then_inc(tile_ready, 1)

            def turn_mem_keys(l):
                for c in range(2):
                    for m in range(2):
                        last = nc.tensor.transpose(banks[:, 6, c * 256 + m * P:c * 256 + (m + 1) * P],
                                                   mkv[:, m, c * P:(c + 1) * P], ident)
                last.then_inc(mkt_t, 1)
                pe.wait_ge(mkt_ready, l + 1)

            pe.wait_ge(tile_free, 4)
            pe.wait_ge(vec_ready, 1)
            turn_mem_keys(0)
            pe.wait_ge(xt_free, KD + 1)
            mean_square(0, sq0)
            pe.wait_ge(xn_ready, 1)
            project_cols(xn, 256, KD)
            pe.wait_ge(xlast_ready, 1)
            for k in range(KD):
                last = nc.tensor.transpose(banks[0:9, 6 + k // 4, (k % 4) * P:(k % 4 + 1) * P], xlast[:, k, :], ident)
            last.then_inc(xlast_t, 1)
            mids = iter(lora_mid)
            for i in range(6):
                pe.wait_ge(mix_ready, i + 1)
                if i in (1, 4, 5):
                    m = P if i == 5 else 64
                    project(take(), 0, m, xmix[i % 2], KD)
                    w = take()
                    mid = next(mids)
                    pe.wait_ge(tile_free, tile[0])
                    for c in range(CM):
                        project(w, c * P, P, mid.unsqueeze(1), 1, m)
                else:
                    project_cols(xmix[i % 2], MIX, KD)
            pe.wait_ge(kk_sq, 1)
            for c in range(CM):
                project(const("pair").unsqueeze(1), 0, P, TMP[:, c:c + 1, :], 1)
            pe.wait_ge(rk_ready, 1)
            for c in range(CM):
                project(const("pair").unsqueeze(1), 0, P, BON[:, c:c + 1, :], 1)

            def pairs(bank, lhs, rhs):
                for c in range(CM):
                    for i in range(2):
                        last = mm(banks[hp(i), bank, c * C:(c + 1) * C], lhs(c, i), rhs(c, i), start=True, stop=True)
                return last

            pe.wait_ge(tile_free, tile[0])
            pe.wait_ge(factors_ready, 1)
            ny = 0
            nx = 0
            for grp in groups:
                for i, j in enumerate(grp):
                    pairs(4 * i, lambda c, q: KK[hp(q), c, cols(j)],
                          lambda c, q: A[hp(q), c, cols(j)]).then_inc(inv_l, 1)
                for lev in range(levels(grp[0])):
                    for i, j in enumerate(grp):
                        nx += 1
                        pe.wait_ge(inv_x, nx)
                        pairs(4 * i, lambda c, q: inv_bufs[i][1][hp(q), c, :],
                              lambda c, q: xt_all[j][hp(q), c, :]).then_inc(inv_y, 1)
                    for i, j in enumerate(grp):
                        ny += 1
                        pe.wait_ge(inv_ysb, ny)
                        pairs(4 * i + 1, lambda c, q: inv_bufs[i][3][hp(q), c, :], lambda c, q: inv_bufs[i][2][hp(q), c, :])
                        pairs(4 * i + 2, lambda c, q: inv_bufs[i][2][hp(q), c, :],
                              lambda c, q: inv_bufs[i][3][hp(q), c, :]).then_inc(inv_d, 1)
                nx += len(grp)
            pe.wait_ge(inv_x, nx)
            pe.wait_ge(s0_in, 16 * CM)

            def turn_states(bank, src, ready, free):
                for c in range(CM):
                    if c >= 2:
                        pe.wait_ge(free, c - 1)
                    for i in range(2):
                        for b in range(NB):
                            last = mm(banks[hp(i), bank + c % 2, b * HD:(b + 1) * HD], src(b, c, i), ident[hp(i), hp(i)],
                                      start=True, stop=True)
                    last.then_inc(ready, 1)

            turn_states(0, lambda b, c, i: s0_raw[hp(i), b, c, :], s0_t, s0_ready)
            pe.wait_ge(s0_ready, CM)
            nturn = [0]

            def turn(lhs):
                n = nturn[0]
                nturn[0] += 1
                if n >= 3:
                    pe.wait_ge(turned_out, n - 2)
                pairs(n % 3, lhs, lambda c, q: ident[hp(q), hp(q)]).then_inc(turned, 1)

            def prepare(n, j):
                for x in (A, K, V):
                    turn(lambda c, q: x[hp(q), c, cols(j)])
                for m, (a, b) in enumerate(((K, KK), (A, R), (K, R))):
                    if n:
                        pe.wait_ge(intra_out, 3 * (n - 1) + m + 1)
                    pairs(3 + m, lambda c, q: a[hp(q), c, cols(j)], lambda c, q: b[hp(q), c, cols(j)]).then_inc(intra, 1)

            def group(out, terms):
                for m, (a, b) in enumerate(terms):
                    last = mm(out, a, b, start=(m == 0), stop=(m == len(terms) - 1))
                return last

            prepare(0, order[0])
            for n, j in enumerate(order):
                B_, K_, V_, Lak, Lrb, Lrk = prep[n % 2]
                sample = j == SAMPLE
                pe.wait_ge(turned_out, nturn[0])
                pe.wait_ge(intra_out, 3 * (n + 1))
                if n:
                    pe.wait_ge(s_new, n)

                def from_state(c, i, chan):
                    if sample:
                        return [(masked[hp(i), c, b, :], s0t[hp(i), c, b, :]) for b in range(NB)]
                    return [(chan[hp(i), c, cols(j)], state[hp(i), n % 2, c, :])]

                def outputs_of_chunk():
                    for c in range(CM):
                        for i in range(2):
                            last = group(banks[hp(i), 7, c * C:(c + 1) * C],
                                         from_state(c, i, R) + [(Lrb[hp(i), c, :], sa_buf[hp(i), c, :]),
                                                                (Lrk[hp(i), c, :], V_[hp(i), c, :])])
                    last.then_inc(o_psum, 1)

                if sample:
                    pe.wait_ge(masked_ready, 1)
                for c in range(CM):
                    for i in range(2):
                        last = group(banks[hp(i), 6, c * C:(c + 1) * C],
                                     from_state(c, i, KK) + [(Lak[hp(i), c, :], V_[hp(i), c, :])])
                last.then_inc(u_psum, 1)
                if n + 1 < NCH and not sample:
                    prepare(n + 1, order[n + 1])
                pe.wait_ge(u_sb, n + 1)
                if n:
                    pe.wait_ge(o_sb, n)
                pairs(7, lambda c, q: xt_all[j][hp(q), c, :], lambda c, q: u_buf[hp(q), c, :]).then_inc(sa_psum, 1)
                if n:
                    pe.wait_ge(on_ready, n)
                    turn(lambda c, q: on_buf[(n - 1) % 2][hp(q), c, :])
                pe.wait_ge(sa_sb, n + 1)
                if sample:
                    pe.wait_ge(masked_ready, 2)
                    outputs_of_chunk()
                    for q, tok in enumerate((B_, K_)):
                        pe.wait_ge(masked_ready, 3 + q)
                        for c in range(CM):
                            m = q * CM + c
                            if m >= 2:
                                pe.wait_ge(dsm_free, m - 1)
                            for i in range(2):
                                last = mm(banks[hp(i), 4 + m % 2, :], tok[hp(i), c, :],
                                          masked[hp(i), c, :, :].rearrange("p b v -> p (b v)"), start=True, stop=True)
                            last.then_inc(dsm_psum, 1)
                    pe.wait_ge(s0_scaled, 1)
                    turn_states(4, lambda b, c, i: s0t[hp(i), c, b, :], st_t, st_out)
                    pe.wait_ge(st_out, CM)
                    prepare(n + 1, order[n + 1])
                else:
                    for c in range(CM):
                        for i in range(2):
                            last = group(banks[hp(i), 6, c * C:(c + 1) * C],
                                         [(B_[hp(i), c, :], sa_buf[hp(i), c, :]), (K_[hp(i), c, :], V_[hp(i), c, :])])
                    last.then_inc(ds_psum, 1)
                    outputs_of_chunk()
            pe.wait_ge(on_ready, NCH)
            turn(lambda c, q: on_buf[(NCH - 1) % 2][hp(q), c, :])
            pe.wait_ge(s_new, NCH)
            pairs(6, lambda c, q: state[hp(q), NCH % 2, c, :], lambda c, q: ident[hp(q), hp(q)]).then_inc(st_t, 1)
            pe.wait_ge(turned_out, nturn[0])
            pe.wait_ge(st_out, CM + 1)

            nt = [0]
            nq = [0]

            def turn_blocks(blocks):
                n = nt[0]
                nt[0] += 1
                if n >= 2:
                    pe.wait_ge(sm_pt, n - 1)
                for src, c0 in blocks:
                    m, w = src.shape[0], src.shape[1]
                    last = nc.tensor.transpose(banks[0:w, 6 + n % 2, c0:c0 + m], src, ident[0:m, 0:m])
                last.then_inc(sm_t, 1)

            def window_keys(i):
                for c0, tiles_ in ((0, range(0, 4)), (1, range(0, 4)), (0, range(4, 8)), (1, range(4, 8))):
                    turn_blocks([(k_dil[:, t_, c0 * P:(c0 + 1) * P], m * P) for m, t_ in enumerate(tiles_)])
                turn_blocks([(k_dil[:, 8, c0 * P:(c0 + 1) * P], c0 * P) for c0 in range(2)])

            seen = {"vals": 0, "keys": 0}

            def scores(l, q, kind, x, hd):
                a = att[l]
                s = 3 * (q % 2)
                c, i = hd // 2, hd % 2
                if q >= 2:
                    pe.wait_ge(sm_cat, q - 1)
                if kind == "mem_p":
                    last = mm(banks[:, s, 0:MEMT], qmem[hp(i), c, x * P:(x + 1) * P], mkt[hp(i), c, :], start=True, stop=True)
                elif kind == "dil_p":
                    tok = slice(x, TP, 4)
                    mm(banks[:, s, 0:TP], qc[hp(i), c, tok], kc[hp(i), c, 0:TP], start=True, stop=True)
                    for g in (1, 2):
                        last = mm(banks[:, s + 1, (g - 1) * P:g * P], qc[hp(i), 2 * g + c, tok], kc[hp(i), 2 * g + c, tok],
                                  start=True, stop=True)
                elif kind == "mem_s":
                    seen["vals"] += 2
                    pe.wait_ge(vals_in, 16 * seen["vals"])
                    for b in range(2):
                        turn_blocks([(a["kv"][b][:, m, c * P:(c + 1) * P], c * MEMT + m * P) for c in range(2) for m in range(2)])
                    pe.wait_ge(sm_pt, nt[0])
                    for b in range(2):
                        last = group(banks[32 * b:32 * b + 32, s, 0:MEMT],
                                     [(a["qs"][0][:, 2 * x + b, c, :], a["kt"][b][:, c, :]) for c in range(2)])
                else:
                    for b in range(2):
                        seen["keys"] += 6
                        pe.wait_ge(keys_in, 16 * seen["keys"])
                        window_keys(b)
                    pe.wait_ge(sm_pt, nt[0])
                    for b in range(2):
                        def part(bank, c0, n, g, keys):
                            return group(banks[32 * b:32 * b + 32, s + bank, c0:c0 + n],
                                         [(a["qs"][1 + g][:, 2 * x + b, c, :], keys(c)) for c in range(2)])
                        part(0, 0, 512, 1, lambda c: kt_dil[b][:, KT1 + c * 512:KT1 + (c + 1) * 512])
                        part(1, 0, 512, 2, lambda c: kt_dil[b][:, KT2 + c * 512:KT2 + (c + 1) * 512])
                        part(2, 0, P, 0, lambda c: kt_dil[b][:, KT0 + c * P:KT0 + (c + 1) * P])
                        for g in range(3):
                            last = part(2, P + g * NS, NS, g, lambda c: kc[:, 2 * g + c, TP:T])
                last.then_inc(sm_s, 1)

            def weigh(l, q, kind, x, hd):
                a = att[l]
                rows = ROWS[kind]
                s = 3 * (q % 2) + 2
                c, i = hd // 2, hd % 2
                pe.wait_ge(sm_p, q + 1)
                for blocks in TURNS[kind]:
                    turn_blocks([(a["p"][q % 2][0:rows, k0:k0 + w], m * rows) for m, (k0, w) in enumerate(blocks)])
                pe.wait_ge(sm_pt, nt[0])
                pt = a["pt"][q % 2]

                def ptb(m, w=P):
                    return pt[0:w, m * rows:(m + 1) * rows]

                if kind == "mem_p":
                    last = group(banks[hp(i), s, 0:P], [(mkv[:, m, 256 + hd * HD:256 + (hd + 1) * HD], ptb(m)) for m in range(2)])
                elif kind == "dil_p":
                    hc = slice(hd * HD, (hd + 1) * HD)
                    last = group(banks[hp(i), s, 0:P], [(v_tok[:, m, hc], ptb(m)) for m in range(4)]
                                 + [(v_class[:, x, g, hc], ptb(4 + g)) for g in range(2)])
                else:
                    if kind == "dil_s":
                        seen["vals"] += 12
                        pe.wait_ge(vals_in, 16 * seen["vals"])
                    for b in range(2):
                        for c in range(2):
                            q0 = 32 * b + 16 * c
                            cc = slice(c * P, (c + 1) * P)
                            if kind == "mem_s":
                                terms = [(a["kv"][b][:, m, 256 + c * P:256 + (c + 1) * P], ptb(m)[:, q0:q0 + 16]) for m in range(2)]
                            else:
                                terms = [(v_dil[b][:, m, cc], ptb(m)[:, q0:q0 + 16]) for m in range(9)]
                                terms += [(v_new[:, g, cc], ptb(9 + g, NS)[:, q0:q0 + 16]) for g in range(3)]
                            last = group(banks[:, s, q0:q0 + 16], terms)
                last.then_inc(sm_o, 1)

            def attention(l, q0):
                for what, n in turn_order(l):
                    (scores if what == "begin" else weigh)(l, q0 + n, *steps[l][n])

            pe.wait_ge(qs_ready, 1)
            attention(0, 0)
            pe.wait_ge(cat_ready, 1)
            pe.wait_ge(sm_cat, len(steps[0]))
            project_cols(att[0]["cat"], D, KD)

            def feed_forward(l, norm, xcount):
                mean_square(norm, sq)
                mean_square(norm + 1, sq)
                pe.wait_ge(xn_ready, xcount)
                project_cols(xf, 2 * FF, KD)
                pe.wait_ge(f_ready, KF * (l + 1))
                project_cols(ff, D, KF, P)
                mean_square(norm + 2, sq)

            feed_forward(0, 1, 2)
            pe.wait_ge(kv_back, 16)
            turn_mem_keys(1)
            mean_square(4, sq)
            pe.wait_ge(xn_ready, 3)
            project_cols(xkv, 2 * MIX, KD)
            project_cols(xf, D, KD)
            for x, end in ((qc, END_QKV), (kc, END_QKV)):
                pe.wait_ge(tile_free, end)
                for c in range(CM):
                    project(const("swap").unsqueeze(1), 0, P, x[:, c:c + 1, :], 1)
            pe.wait_ge(rotated, 2)
            for m in range(5):
                tok = slice(m * P, (m + 1) * P) if m < 4 else slice(TP, T)
                rows_ = [x[:, c, tok] for x in (kc, vc) for c in range(CM)]
                for q in range(3):
                    turn_blocks([(r, n * P) for n, r in enumerate(rows_[4 * q:4 * q + 4])])
            for r in range(4):
                turn_blocks([(vc[:, CM // 3 + n, slice(r, TP, 4)], n * P) for n in range(4)])
            pe.wait_ge(qs_ready, 2)
            pe.wait_ge(v_copied, 1)
            attention(1, len(steps[0]))
            pe.wait_ge(sm_cat, len(steps[0]) + len(steps[1]))
            project_cols(att[1]["cat"], D, 4)
            feed_forward(1, 5, 4)
            pe.wait_ge(h_ready, 4)
            for k in range(4):
                for q in range(2):
                    turn_blocks([(h[:, 4 * q + n, k * P:(k + 1) * P], n * P) for n in range(4)])
            for q in range(2):
                turn_blocks([(h[:, 4 * q + n, TP:T], n * P) for n in range(4)])

        @block.scalar
        def _(act):
            f = nc.scalar.activation
            tile = [0]
            chain = [0]

            def link(ins):
                chain[0] += 1
                ins.then_inc(achain, 1)
                act.wait_ge(achain, chain[0])

            def drain_tile(out, func, m=P, **kw):
                n = tile[0]
                tile[0] += 1
                act.wait_ge(tile_ready, n + 1)
                f(halves(out), bankpair(n, m), func, **kw).then_inc(tile_free, 1)

            def norm_scale(n, src, squares):
                f(flat(squares), flat(src), ACT.Square).then_inc(sq_ready, 1)
                act.wait_ge(ms_ready, n + 1)
                link(f(halves(ln_ms), banks[:, 6:8, 0:HALF], ACT.Ln, bias=const("eps")))
                f(rstd, ln_ms, ACT.Exp, scale=-0.5).then_inc(rstd_ready, 1)

            act.wait_ge(consts_in, 16)
            act.wait_ge(mem_in, 16)
            for m in range(2):
                last = f(at(A_XN + m * D, D), mem_tok[:, m, :], ACT.Square, accum_out=small[:, m:m + 1])
            link(last)
            link(f(small[:, 2:4], small[:, 0:2], ACT.Ln, bias=const("eps"), scale=1.0 / D))
            link(f(small[:, 4:6], small[:, 2:4], ACT.Exp, scale=-0.5))
            for m in range(2):
                f(mem_tok[:, m, :], mem_tok[:, m, :], ACT.Copy, scale=small[:, 4 + m:5 + m]).then_inc(mem_scaled, 1)
            act.wait_ge(vec_t, 1)
            f(vec[:, 0:CM, :], banks[:, 6, 0:CM * NVEC].rearrange("p (k n) -> p k n", k=CM), ACT.Copy)
            f(vec[:, CM:KD, 0:NVEC_D], banks[:, 6, CM * NVEC:KD * NVEC].rearrange("p (k n) -> p k n", n=NVEC)[:, :, 0:NVEC_D],
              ACT.Copy).then_inc(vec_ready, 1)
            for q in range(4):
                act.wait_ge(mt_ready, q + 1)
                f(flat(mem_t[:, 2 * q:2 * q + 2, :]), banks[:, q, :], ACT.Copy).then_inc(mt_free, 1)
            for k in range(KD):
                act.wait_ge(xt_ready, k + 1)
                f(h0[:, k, 0:TP], banks[:, 4 + k % 2, :], ACT.Copy).then_inc(xt_free, 1)
            act.wait_ge(xt_ready, KD + 1)
            f(h0[:, :, TP:T], banks[:, 7, :].rearrange("p (k n) -> p k n", k=KD), ACT.Copy).then_inc(xt_free, 1)
            for l in range(2):
                for u in range(2):
                    for m in range(2):
                        n = tile[0]
                        tile[0] += 1
                        act.wait_ge(tile_ready, n + 1)
                        f((mkv[:, :, :], mkv1)[l][:, m, u * 256:(u + 1) * 256], banks[:, 2 * (n % 3), 0:256], ACT.Copy).then_inc(tile_free, 1)

            def mem_keys(l):
                act.wait_ge(mkt_t, l + 1)
                f(mkt[:, :, :].rearrange("p a b -> p (a b)"), banks[:, 6, :], ACT.Copy).then_inc(mkt_ready, 1)

            mem_keys(0)
            act.wait_ge(xt_free, KD + 1)
            norm_scale(0, h0, sq0)
            for c in range(2):
                drain_tile(qmem[:, c, :], ACT.Copy)
            act.wait_ge(xlast_t, 1)
            f(shift_out.rearrange("p (a b) -> p a b", a=2), banks[0:9, 6:8, :], ACT.Copy).then_inc(shift_ready, 1)
            for c in range(CM):
                drain_tile(R[:, c, :], ACT.Copy)
            drain_tile(lora_mid[0][0:64, :], ACT.Tanh, m=64)
            act.wait_ge(phase_a_stored, 16 * 5)
            for c in range(CM):
                drain_tile(LW[:, c, :], ACT.Sigmoid, bias=vec[:, c, W0:W0 + 1])
            for buf in (K, V):
                for c in range(CM):
                    drain_tile(buf[:, c, :], ACT.Copy)
            drain_tile(lora_mid[1][0:64, :], ACT.Copy, m=64)
            for c in range(CM):
                drain_tile(A[:, c, :], ACT.Sigmoid, bias=vec[:, c, A0:A0 + 1])
            drain_tile(lora_mid[2], ACT.Sigmoid)
            for c in range(CM):
                drain_tile(G[:, c, :], ACT.Copy)
            act.wait_ge(kk_ready, 1)
            f(flat(TMP), flat(KK), ACT.Square).then_inc(kk_sq, 1)
            for c in range(CM):
                drain_tile(CL[:, c, :], ACT.Copy)
            act.wait_ge(ss_clamped, 1)
            link(f(flat(TMP), flat(CL), ACT.Ln, scale=2.0 ** 20))
            f(flat(CL), flat(TMP), ACT.Exp, scale=-0.5, bias=const("ln_shift")).then_inc(kk_scale, 1)
            act.wait_ge(kk_scale, 1)
            for c in range(CM):
                drain_tile(TMP[:, c, :], ACT.Copy)
            act.wait_ge(cum_ready, 1)
            f(flat(TMP), flat(CL), ACT.Exp).then_inc(grown, 1)
            act.wait_ge(shifted, 1)
            f(flat(LW), flat(LW), ACT.Exp).then_inc(grown, 1)
            act.wait_ge(grown_used, 1)
            f(flat(TMP), flat(CL), ACT.Exp, scale=-1.0).then_inc(shrunk, 1)

            nl = ny = 0
            for grp in groups:
                for i, j in enumerate(grp):
                    nl += 1
                    act.wait_ge(inv_l, nl)
                    f(flat(inv_bufs[i][0]), banks[:, 4 * i, 0:CM * C], ACT.Copy).then_inc(inv_lsb, 1)
                for lev in range(levels(grp[0])):
                    for i, j in enumerate(grp):
                        ny += 1
                        act.wait_ge(inv_y, ny)
                        f(flat(inv_bufs[i][3]), banks[:, 4 * i, 0:CM * C], ACT.Copy).then_inc(inv_ysb, 1)
            for c in range(CM):
                act.wait_ge(s0_t, c + 1)
                f(s0t[:, c, :, :].rearrange("p b v -> p (b v)"), banks[:, c % 2, :], ACT.Copy).then_inc(s0_ready, 1)
            nturn = [0]

            def turned_to(dst, to_chunk=None):
                n = nturn[0]
                nturn[0] += 1
                act.wait_ge(turned, n + 1)
                f(dst, banks[:, n % 3, 0:CM * C].rearrange("p (c v) -> p c v", c=CM), ACT.Copy).then_inc(turned_out, 1)

            def prepare(n):
                for m in range(3):
                    turned_to(prep[n % 2][m])

            prepare(0)
            for n, j in enumerate(order):
                act.wait_ge(u_psum, n + 1)
                f(flat(u_buf), banks[:, 6, 0:CM * C], ACT.Copy).then_inc(u_sb, 1)
                if n:
                    act.wait_ge(var_ready, n)
                    link(f(small[:, 24:30], small[:, 18:24], ACT.Ln, scale=1.0 / HD, bias=const("lnx_eps")))
                    f(small[:, 30:36], small[:, 24:30], ACT.Exp, scale=-0.5).then_inc(gn_ready, 1)
                    if n + 1 < NCH:
                        prepare(n + 1)
                act.wait_ge(sa_psum, n + 1)
                f(flat(sa_buf), banks[:, 7, 0:CM * C], ACT.Copy).then_inc(sa_sb, 1)
                if n:
                    turned_to(R[:, :, cols(order[n - 1])])
                if n >= 2:
                    act.wait_ge(on_ready, n - 1)
                act.wait_ge(o_psum, n + 1)
                f(flat(o_buf[n % 2]), banks[:, 7, 0:CM * C], ACT.Copy).then_inc(o_sb, 1)
                if not n:
                    for c in range(CM):
                        act.wait_ge(st_t, c + 1)
                        f(s0_raw[:, :, c, :], banks[:, 4 + c % 2, :].rearrange("p (b k) -> p b k", b=NB), ACT.Copy).then_inc(st_out, 1)
                    prepare(1)
            act.wait_ge(var_ready, NCH)
            link(f(small[:, 24:30], small[:, 18:24], ACT.Ln, scale=1.0 / HD, bias=const("lnx_eps")))
            f(small[:, 30:36], small[:, 24:30], ACT.Exp, scale=-0.5).then_inc(gn_ready, 1)
            turned_to(R[:, :, cols(order[-1])])
            act.wait_ge(st_t, CM + 1)
            f(flat(prep[0][0]), banks[:, 6, 0:CM * C], ACT.Copy).then_inc(st_out, 1)

            nt = [0]

            def turned_blocks(dst, c0, n, m=P, **kw):
                b = nt[0]
                nt[0] += 1
                act.wait_ge(sm_t, b + 1)
                src = banks[0:m, 6 + b % 2, c0:c0 + n]
                return f(dst, src, ACT.Copy).then_inc(sm_pt, 1)

            def exps(l, q, kind, x, hd):
                rows, w = ROWS[kind], WIDTH[kind]
                act.wait_ge(sm_max, q + 1)
                if q >= 2:
                    act.wait_ge(sm_o, q - 1)
                k = 40 + 2 * (q % 2)
                f(att[l]["p"][q % 2][0:rows, 0:w], banks3(q)[0:rows, 0:w],
                  ACT.Exp, scale=SCALE, bias=small[0:rows, k:k + 1], accum_out=small[0:rows, k + 1:k + 2]).then_inc(sm_exp, 1)

            def keys(l, kind):
                if kind == "mem_s":
                    for b in range(2):
                        turned_blocks(flat(att[l]["kt"][b]), 0, 512)
                elif kind == "dil_s":
                    for b in range(2):
                        for k0 in (KT1, KT1 + 512, KT2, KT2 + 512):
                            turned_blocks(kt_dil[b][:, k0:k0 + 512], 0, 512)
                        turned_blocks(kt_dil[b][:, KT0:KT0 + 256], 0, 256)

            def attention(l, q0):
                for what, n in turn_order(l):
                    st = steps[l][n]
                    if what == "begin":
                        keys(l, st[0])
                        exps(l, q0 + n, *st)
                        continue
                    rows = ROWS[st[0]]
                    pt = att[l]["pt"][(q0 + n) % 2]
                    at_ = 0
                    for blocks in TURNS[st[0]]:
                        full = [b for b in blocks if b[1] == P]
                        part = len(blocks) - len(full)
                        w = len(full) * rows
                        if not part:
                            turned_blocks(pt[:, at_:at_ + w], 0, w)
                        else:
                            b = nt[0]
                            nt[0] += 1
                            act.wait_ge(sm_t, b + 1)
                            f(pt[:, at_:at_ + w], banks[:, 6 + b % 2, 0:w], ACT.Copy)
                            f(pt[0:NS, at_ + w:at_ + w + part * rows], banks[0:NS, 6 + b % 2, w:w + part * rows],
                              ACT.Copy).then_inc(sm_pt, 1)
                        at_ += len(blocks) * rows

            attention(0, 0)

            def mixed(norm):
                for c in range(KD):
                    drain_tile(y[:, c, :], ACT.Copy)
                act.wait_ge(tile_free, tile[0])
                norm_scale(norm, y, sq)

            def feed_forward(l, norm):
                mixed(norm)
                act.wait_ge(h_ready, 2 * l + 1)
                norm_scale(norm + 1, h, sq)
                for u in range(FF // 256):
                    for i in range(2):
                        drain_tile(ff[:, 2 * u + i, :], ACT.Silu)
                    for i in range(2):
                        m = 2 * u + i + KF * l
                        if m >= 2:
                            act.wait_ge(f_ready, m - 1)
                        n = tile[0]
                        tile[0] += 1
                        act.wait_ge(tile_ready, n + 1)
                        f(halves(up[:, i, :]), bankpair(n), ACT.Copy).then_inc(tile_free, 1)
                mixed(norm + 2)

            feed_forward(0, 1)
            mem_keys(1)
            act.wait_ge(h_ready, 2)
            norm_scale(4, h, sq)
            for buf in (kc, vc, qc):
                for c in range(CM):
                    drain_tile(buf[:, c, :], ACT.Copy)
            for c in range(2):
                drain_tile(qmem[:, c, :], ACT.Copy)
            for buf in rot:
                for c in range(CM):
                    drain_tile(buf[:, c, :], ACT.Copy)
            for m in range(5):
                for q in range(3):
                    b = nt[0]
                    nt[0] += 1
                    act.wait_ge(sm_t, b + 1)
                    if m < 4:
                        dst = kv_tok[:, m, :, :].rearrange("p k n -> p (k n)")[:, q * 512:(q + 1) * 512]
                    else:
                        dst = kv_new.rearrange("p k n -> p (k n)")[:, q * 512:(q + 1) * 512]
                    f(dst, banks[0:(P if m < 4 else NS), 6 + b % 2, :], ACT.Copy).then_inc(sm_pt, 1)
            for r in range(4):
                turned_blocks(v_class[:, r, :, :].rearrange("p g n -> p (g n)"), 0, 512)
            act.wait_ge(v_copied, 1)
            act.wait_ge(kv_stored, KV_STORES * 16)
            attention(1, len(steps[0]))
            feed_forward(1, 5)
            for k in range(4):
                for q in range(2):
                    turned_blocks(y_tok[:, k, q * 512:(q + 1) * 512], 0, 512)
            for q in range(2):
                turned_blocks(y_new[:, q * 512:(q + 1) * 512], 0, 512, m=NS)

        @block.vector
        def _(dve):
            v = nc.vector
            chain = [0]

            def link(ins):
                chain[0] += 1
                ins.then_inc(vchain, 1)
                dve.wait_ge(vchain, chain[0])

            dve.wait_ge(consts_in, 16)
            v.memset(state[:, 1], 0.0).then_inc(s_new, 1)
            dve.wait_ge(mt_free, 4)
            dve.wait_ge(vec_ready, 1)
            for l in range(2):
                v.tensor_tensor(mem_g[:, l], mem_t, each(vec[:, :, G_MEM + l], MEMT), ALU.mult).then_inc(mem_g_ready, 1)

            def normed(dst, src, g, last_sem, n=KD):
                for k in range(n):
                    ins = v.scalar_tensor_tensor(dst[:, k, :], src[:, k, :], vec[:, k, g:g + 1], rstd, ALU.mult, ALU.mult)
                ins.then_inc(last_sem, 1)

            dve.wait_ge(rstd_ready, 1)
            normed(xn, h0, G_PRE, xn_ready)
            dve.wait_ge(xn_ready, 1)
            v.tensor_tensor(xd[:, :, 1:TP], xn[:, :, 0:TP - 1], xn[:, :, 1:TP], ALU.subtract)
            v.tensor_scalar(xd[:, :, 0:1], xn[:, :, 0:1], -1.0, None, ALU.mult)
            xns, xds = [a[:, :, TP:T].rearrange("p k (b t) -> p k b t", b=NB) for a in (xn, xd)]
            v.tensor_tensor(xds[:, :, :, 1:TS], xns[:, :, :, 0:TS - 1], xns[:, :, :, 1:TS], ALU.subtract)
            v.tensor_tensor(xds[:, :, :, 0], vec[:, :, SHIFT:SHIFT + NB], xns[:, :, :, 0], ALU.subtract)
            v.tensor_copy(xlast[:, :, 0:1], xn[:, :, TP - 1:TP])
            link(v.tensor_copy(xlast[:, :, 1:9], xns[:, :, :, TS - 1]))
            v.tensor_copy(small[:, 36:37], const("eps")).then_inc(xlast_ready, 1)
            ends = (END_R, END_W1, END_K, END_V)
            for i in range(6):
                if i >= 2:
                    dve.wait_ge(tile_ready, ends[i - 2])
                if i == 1:
                    dve.wait_ge(h_saved, 16)
                for k in range(KD):
                    ins = v.scalar_tensor_tensor(xmix[i % 2][:, k, :], xd[:, k, :], vec[:, k, MU + i:MU + i + 1],
                                                 xn[:, k, :], ALU.mult, ALU.add)
                ins.then_inc(mix_ready, 1)
            dve.wait_ge(tile_free, END_PROJ)
            for c in range(CM):
                ins = v.tensor_scalar(KK[:, c, :], K[:, c, :], vec[:, c, K_K:K_K + 1], None, ALU.mult)
            ins.then_inc(kk_ready, 1)
            link(v.tensor_scalar(flat(LW), flat(LW), -float(2.718281828459045 ** -0.5), None, ALU.mult))
            for c in range(CM):
                ins = v.tensor_scalar(BON[:, c, :], A[:, c, :], 1.0, vec[:, c, K_A:K_A + 1], ALU.subtract, ALU.mult)
            link(ins)
            link(v.scalar_tensor_tensor(flat(K), flat(BON), 1.0, flat(K), ALU.add, ALU.mult))
            for c in range(CM):
                ins = v.scalar_tensor_tensor(BON[:, c, :], R[:, c, :], vec[:, c, R_K:R_K + 1], K[:, c, :], ALU.mult, ALU.mult)
            ins.then_inc(rk_ready, 1)
            dve.wait_ge(tile_free, END_PROJ + CM)
            v.tensor_scalar(flat(CL), flat(CL), 1e-24, None, ALU.max).then_inc(ss_clamped, 1)
            dve.wait_ge(kk_scale, 1)
            link(v.tensor_tensor(flat(KK), flat(KK), flat(CL), ALU.mult))
            v.tensor_tensor(flat(A), flat(A), flat(KK), ALU.mult)
            for c in range(CM):
                ins = v.tensor_tensor_scan(CL[:, c, :], const("carry"), LW[:, c, :], 0.0, ALU.mult, ALU.add)
            link(ins)
            dve.wait_ge(tile_free, END_PROJ + 2 * CM)
            link(v.tensor_tensor(flat(BON), flat(TMP), flat(V), ALU.mult))
            v.tensor_copy(small[:, 37:38], const("eps")).then_inc(cum_ready, 1)
            v.tensor_tensor(flat(LW), flat(CL), flat(LW), ALU.subtract).then_inc(shifted, 1)
            dve.wait_ge(grown, 1)
            v.tensor_copy(decay_end[:, :, 0:8], TMP[:, :, C - 1:TP:C])
            v.tensor_copy(decay_end[:, :, 8:16], TMP[:, :, TP + TS - 1:T:TS])
            v.tensor_tensor(flat(R), flat(R), flat(TMP), ALU.mult).then_inc(grown_used, 1)
            dve.wait_ge(grown, 2)
            link(v.scalar_tensor_tensor(flat(KK), flat(KK), -1.0, flat(LW), ALU.mult, ALU.mult))
            dve.wait_ge(shrunk, 1)
            v.tensor_tensor(flat(A), flat(A), flat(TMP), ALU.mult)
            v.tensor_tensor(flat(K), flat(K), flat(TMP), ALU.mult).then_inc(factors_ready, 1)

            def level(n):
                a = CONSTS["level"][0] + n * C
                return over(consts[:, a:a + C], CM)

            def bank6(b):
                return banks[:, b, 0:CM * C].rearrange("p (c v) -> p c v", c=CM)

            nl = nd = 0
            dve.wait_ge(factors_ready, 1)
            for grp in groups:
                if nl:
                    dve.wait_ge(inv_x, nl + nd)
                for i, j in enumerate(grp):
                    nl += 1
                    v.tensor_copy(inv_bufs[i][2], over(const("ids"), CM))
                    v.tensor_copy(xt_all[j], over(const("ids"), CM))
                    dve.wait_ge(inv_lsb, nl)
                    v.tensor_tensor(inv_bufs[i][1], inv_bufs[i][0], level(0), ALU.mult).then_inc(inv_x, 1)
                for lev in range(levels(grp[0])):
                    for i, j in enumerate(grp):
                        nd += 1
                        dve.wait_ge(inv_d, nd)
                        v.tensor_tensor(inv_bufs[i][2], bank6(4 * i + 1), inv_bufs[i][2], ALU.add)
                        if lev + 1 < levels(j):
                            v.tensor_tensor(inv_bufs[i][1], inv_bufs[i][0], level(lev + 1), ALU.mult)
                        v.tensor_tensor(xt_all[j], bank6(4 * i + 2), xt_all[j], ALU.add).then_inc(inv_x, 1)
            dve.wait_ge(s0_t, CM)

            def mask_batches(src, out=masked):
                inb = const("in_batch").rearrange("p (b t) -> p b t", b=NB)
                for c in range(CM):
                    ins = v.tensor_tensor(masked[:, c], src[:, c, TP:T].unsqueeze(1).broadcast_to([P, NB, C]), inb, ALU.mult)
                ins.then_inc(masked_ready, 1)

            def mask_rows(src):
                for c in range(CM):
                    ins = v.tensor_tensor(masked[:, c], over(src[:, c, :], NB), each(const("of_batch"), HD), ALU.mult)
                ins.then_inc(masked_ready, 1)

            def intra_of(n):
                s = order[n] == SAMPLE
                for m, name in enumerate(("before", "upto", "upto")):
                    dve.wait_ge(intra, 3 * n + m + 1)
                    v.tensor_tensor(prep[n % 2][3 + m], bank6(3 + m), over(const(name + ("_s" if s else "")), CM),
                                    ALU.mult).then_inc(intra_out, 1)

            def centre(n):
                o = o_buf[n % 2]
                dve.wait_ge(o_sb, n + 1)
                link(v.tensor_reduce(small[:, 6:12], o, AX_X, ALU.add))
                link(v.tensor_scalar(small[:, 12:18], small[:, 6:12], -1.0 / HD, None, ALU.mult))
                link(v.tensor_tensor(o_centred, o, each(small[:, 12:18], HD), ALU.add))
                link(v.tensor_tensor(on_buf[n % 2], o_centred, o_centred, ALU.mult))
                v.tensor_reduce(small[:, 18:24], on_buf[n % 2], AX_X, ALU.add).then_inc(var_ready, 1)

            def scale_outputs(n):
                dve.wait_ge(gn_ready, n + 1)
                v.tensor_tensor(on_buf[n % 2], o_centred, each(small[:, 30:36], HD), ALU.mult).then_inc(on_ready, 1)

            mask_batches(KK)
            intra_of(0)
            for n, j in enumerate(order):
                if not n:
                    dve.wait_ge(u_psum, 1)
                    mask_batches(R)
                    dve.wait_ge(o_psum, 1)
                    dve.wait_ge(sa_sb, 1)
                    mask_rows(sa_buf)
                    for m in range(2 * CM):
                        if m == CM:
                            dve.wait_ge(dsm_psum, CM)
                            mask_rows(prep[0][2])
                        dve.wait_ge(dsm_psum, m + 1)
                        s = s0t[:, m % CM].rearrange("p b v -> p (b v)")
                        ins = v.tensor_tensor(s, banks[:, 4 + m % 2, :], s, ALU.add)
                        ins.then_inc(dsm_free, 1)
                    dve.wait_ge(dsm_free, 2 * CM)
                    for c in range(CM):
                        ins = v.tensor_tensor(s0t[:, c], s0t[:, c], each(decay_end[:, c, 8:16], HD), ALU.mult)
                    ins.then_inc(s0_scaled, 1)
                    centre(0)
                    dve.wait_ge(st_t, CM)
                    intra_of(1)
                else:
                    scale_outputs(n - 1)
                    if n + 1 < NCH:
                        intra_of(n + 1)
                    dve.wait_ge(ds_psum, n)
                    after = state[:, (n + 1) % 2]
                    link(v.tensor_tensor(after, bank6(6), state[:, n % 2], ALU.add))
                    v.tensor_tensor(after, after, each(decay_end[:, :, j], HD), ALU.mult).then_inc(s_new, 1)
                    centre(n)
            scale_outputs(NCH - 1)
            dve.wait_ge(turned_out, 4 * NCH)
            cat0 = att[0]["cat"]
            for c in range(CM):
                ins = v.tensor_scalar(R[:, c, :], R[:, c, :], vec[:, c, LNX_W:LNX_W + 1], vec[:, c, LNX_B:LNX_B + 1], ALU.mult, ALU.add)
            link(ins)
            link(v.tensor_tensor(flat(R), flat(R), flat(BON), ALU.add))
            v.tensor_tensor(flat(cat0[:, 0:CM, :]), flat(R), flat(G), ALU.mult).then_inc(cat_ready, 1)

            def spread_queries(dst, src):
                link(v.memset(dst, 0.0))
                for c in range(2):
                    for i in range(2):
                        hd = 2 * c + i
                        ins = v.tensor_copy(dst[hp(i), :, c, hd * TS:(hd + 1) * TS],
                                            src[hp(i), c, TP:T].rearrange("p (b t) -> p b t", b=NB))
                return ins

            def maxima(l, q, kind, x, hd):
                rows, w = ROWS[kind], WIDTH[kind]
                s = banks3(q)[0:rows, 0:w]
                k = 40 + 2 * (q % 2)
                m = small[0:rows, 44 + q % 2:45 + q % 2]
                dve.wait_ge(sm_s, q + 1)
                if q >= 2:
                    dve.wait_ge(sm_exp, q - 1)
                if kind == "dil_p":
                    link(v.tensor_tensor(s[:, 0:TP], s[:, 0:TP], mask_p[:, x * TP:(x + 1) * TP], ALU.add))
                    link(v.tensor_tensor(s[:, TP:w], s[:, TP:w], mask_p[:, 4 * TP:4 * TP + 2 * P], ALU.add))
                elif kind == "dil_s":
                    link(v.tensor_tensor(s[:, 0:1152], s[:, 0:1152], mask_s[:, 0:1152], ALU.add))
                    link(v.tensor_tensor(s[:, 1152:w], s[:, 1152:w], mask_s[:, 1152 + x * 192:1152 + (x + 1) * 192], ALU.add))
                link(v.tensor_reduce(m, s, AX_X, ALU.max))
                v.tensor_scalar(small[0:rows, k:k + 1], m, -SCALE, None, ALU.mult).then_inc(sm_max, 1)

            def normalise(l, q, kind):
                rows, w = ROWS[kind], WIDTH[kind]
                k = 40 + 2 * (q % 2)
                p = att[l]["p"][q % 2][0:rows, 0:w]
                r = small[0:rows, 46 + q % 2:47 + q % 2]
                dve.wait_ge(sm_exp, q + 1)
                link(v.reciprocal(r, small[0:rows, k + 1:k + 2]))
                v.tensor_scalar(p, p, r, None, ALU.mult).then_inc(sm_p, 1)

            def gather(l, q, kind, x, hd):
                a = att[l]
                c, i = hd // 2, hd % 2
                src = banks[:, 3 * (q % 2) + 2, :]
                dve.wait_ge(sm_o, q + 1)
                if kind == "mem_p":
                    v.tensor_copy(a["cat"][hp(i), a["mem_tile"] + c, x * P:(x + 1) * P], src[hp(i), 0:P]).then_inc(sm_cat, 1)
                elif kind == "dil_p":
                    v.tensor_copy(a["cat"][hp(i), c, slice(x, TP, 4)], src[hp(i), 0:P]).then_inc(sm_cat, 1)
                else:
                    c0 = a["mem_tile"] if kind == "mem_s" else 0
                    for c in range(2):
                        for i in range(2):
                            ins = v.tensor_copy(
                                a["cat"][hp(i), c0 + c, TP + 16 * x:TP + 16 * x + 16].rearrange("p (b t) -> p b t", b=2),
                                src[hp(i), 0:64].rearrange("p (b c i t) -> p b c i t", b=2, c=2, i=2)[:, :, c, i, :])
                    ins.then_inc(sm_cat, 1)

            def attention(l, q0):
                for what, n in turn_order(l):
                    st = steps[l][n]
                    if what == "begin":
                        maxima(l, q0 + n, *st)
                    else:
                        normalise(l, q0 + n, st[0])
                        gather(l, q0 + n, *st)

            spread_queries(att[0]["qs"][0], qmem[:, :, :]).then_inc(qs_ready, 1)
            attention(0, 0)

            def add_normed(norm, g, count):
                dve.wait_ge(rstd_ready, norm + 1)
                for k in range(KD):
                    ins = v.scalar_tensor_tensor(y[:, k, :], y[:, k, :], vec[:, k, g:g + 1], rstd, ALU.mult, ALU.mult)
                link(ins)
                v.tensor_tensor(flat(h), flat(h), flat(y), ALU.add).then_inc(h_ready, 1)

            def feed_forward(l, norm):
                dve.wait_ge(h_back, 16 * (l + 1))
                add_normed(norm, G_POST + l, 0)
                dve.wait_ge(rstd_ready, norm + 2)
                normed(xf, h, G_PRE_F + l, xn_ready)
                for u in range(FF // 256):
                    for i in range(2):
                        n = END_UP[l] + 4 * u + 2 + i + 1
                        dve.wait_ge(tile_free, n)
                        m = 2 * u + i
                        v.tensor_tensor(ff[:, m, :], ff[:, m, :], up[:, i, :], ALU.mult).then_inc(f_ready, 1)
                add_normed(norm + 2, G_POST_F + l, 0)

            END_UP = (END_OUT0, END_OUT1)
            feed_forward(0, 1)
            dve.wait_ge(rstd_ready, 5)
            for k in range(KD):
                v.scalar_tensor_tensor(xkv[:, k, :], h[:, k, :], vec[:, k, G_KV:G_KV + 1], rstd, ALU.mult, ALU.mult)
            normed(xf, h, G_PRE + 1, xn_ready)
            dve.wait_ge(cos_in, 16)
            for n, x in enumerate((qc, kc)):
                dve.wait_ge(tile_free, END_QKV + CM * (n + 1))
                v.tensor_tensor(x, x, over(cos_sin[:, 0, :], CM), ALU.mult)
                link(v.tensor_tensor(rot[n], rot[n], over(cos_sin[:, 1, :], CM), ALU.mult))
                v.tensor_tensor(x, x, rot[n], ALU.add).then_inc(rotated, 1)
            dve.wait_ge(rotated, 1)
            dve.wait_ge(sm_pt, NT0 + 15 + 4)
            dve.wait_ge(h_saved, 32)
            for g in range(3):
                spread_queries(att[1]["qs"][1 + g], qc[:, 2 * g:2 * g + 2, :])
            spread_queries(att[1]["qs"][0], qmem[:, :, :]).then_inc(qs_ready, 1)
            v.tensor_copy(v_tok, kv_tok[:, :, 1, 0:256])
            v.tensor_copy(v_new, kv_new[:, 1, :].rearrange("p (g n) -> p g n", g=3)).then_inc(v_copied, 1)
            dve.wait_ge(masks_in, 32)
            attention(1, len(steps[0]))
            feed_forward(1, 5)


_OUTS = [(1, TP, D), (NB, TS, D), (1, 1, 12, HD, HD), (1, 1, D), (1, 128, 2, 4, HD), (1, 512, 2, 4, HD),
         (1, 1024, 2, 4, HD), (2, 1, 256, 2, 4, HD), (1, NB, 12, HD, HD), (1, NB, D), (NB, 128, 2, 4, HD),
         (NB, 512, 2, 4, HD), (NB, 1024, 2, 4, HD)]
_UNUSED = ("a_v0", "a_v1", "a_v2")


def constants():
    import numpy as np

    f = np.float32
    p = np.arange(P)
    out = np.zeros((P, NCONST), f)

    def put(name, v):
        a, b = CONSTS[name]
        out[:, a:b] = v

    put("ident", np.eye(P))
    put("mean", np.full((P, P), 1.0 / D))
    put("pair", p[:, None] // HD == p[None] // HD)
    swap = np.zeros((P, P))
    for to in range(P):
        d = to % HD
        swap[to + HD // 2 if d < HD // 2 else to - HD // 2, to] = -1.0 if d < HD // 2 else 1.0
    put("swap", swap)
    t = np.arange(T)
    put("carry", np.broadcast_to(np.where(t < TP, t % C != 0, (t - TP) % TS != 0), (P, T)))
    s, q = (p % C)[:, None], np.arange(C)[None]
    put("before", s < q)
    put("upto", s <= q)
    put("before_s", (s < q) & (s // TS == q // TS))
    put("upto_s", (s <= q) & (s // TS == q // TS))
    put("level", np.concatenate([(((s >> n) & 1) == 1) & ((q >> n) == (s >> n) - 1) for n in range(LEVELS)], 1))
    put("ids", s == q)
    put("in_batch", np.broadcast_to((np.arange(NB)[:, None] == (np.arange(C) // TS)[None]).reshape(-1), (P, NB * C)))
    put("of_batch", s // TS == np.arange(NB)[None])
    put("eps", 1e-6)
    put("lnx_eps", HD * 1e-5)
    put("ln_shift", 10 * np.log(2.0))

    half = HD // 2
    inv = f(10000.0) ** (-np.arange(half, dtype=f) / f(half))
    pos = np.concatenate([np.arange(TP), 1024 + np.tile(np.arange(TS), NB)]).astype(f)
    ang = pos[:, None] * inv[None]
    cs = np.stack([np.cos(ang), np.sin(ang)], 0).astype(f)
    cos_sin = np.ascontiguousarray(cs.transpose(2, 0, 1)[p % half])

    def bias(ok):
        return np.where(ok, 0.0, NEG).astype(f)

    r = np.arange(4)[None, :, None]
    off = (4 * p[:, None, None] + r) - np.arange(TP)[None, None]
    g0 = bias((off >= 0) & (off <= 128)).reshape(P, 4 * TP)
    du = p[:, None] - p[None]
    mask_p = np.concatenate([g0, bias(du >= 0), bias((du >= 0) & (du % 4 == 0))], 1)
    row = np.arange(64)
    tq, bq = (row % TS)[:, None], (row // 32)[:, None]
    k1, k0, k2 = np.arange(512)[None], np.arange(128)[None], np.arange(512)[None]
    parts = [bias((k1 >= tq) & ((k1 - tq) % 4 == 0)), bias((k2 % TS == tq) & (k2 >= 0)), bias(k0 >= tq)]
    new = np.arange(NS)[None]
    for g in range(NB // 2):
        for dil in (1, 4, 16):
            d = tq - new % TS
            parts.append(bias((new // TS == 2 * g + bq) & (d >= 0) & (d % dil == 0)))
    return {"consts": out, "cos_sin": cos_sin, "mask_p": mask_p.astype(f), "mask_s": np.concatenate(parts, 1).astype(f)}


def kernel(**inputs):
    import numpy as np
    import concourse.bacc as bacc
    from concourse.bass_utils import run_bass_kernel_spmd

    nc = bacc.Bacc("TRN2", target_bir_lowering=False, num_devices=1)
    arrays, ins = {}, {}
    given = {n: a for n, a in inputs.items() if n not in _UNUSED}
    for name, a in {**given, **constants()}.items():
        a = np.ascontiguousarray(a)
        arrays[f"in_{name}"] = a
        ins[name] = nc.dram_tensor(f"in_{name}", a.shape, mybir.dt.from_np(a.dtype), kind="ExternalInput").ap()
    outs = [nc.dram_tensor(f"out_{i}", s, F32, kind="ExternalOutput").ap() for i, s in enumerate(_OUTS)]
    trunk(nc, ins, outs)
    r = run_bass_kernel_spmd(nc, [arrays], core_ids=[0])
    return tuple(r.results[0][f"out_{i}"] for i in range(len(_OUTS)))
```

```python
import math
from contextlib import ExitStack

import concourse.bass as bass
from concourse import mybir

ALU = mybir.AluOpType
ACT = mybir.ActivationFunctionType
F32 = mybir.dt.float32
F32R = mybir.dt.float32r
AX_X = mybir.AxisListType.X

P = 128
D = 1024
KD = D // P
TP, NB, TS = 512, 8, 8
NS = NB * TS
T = TP + NS
HALF = T // 2
HD = 64
MIX = 3 * D // 4
CM = MIX // P
FF = 2816
KF = FF // P
C = 64
NCH = T // C
SAMPLE = NCH - 1
LEVELS = 6
SAMPLE_LEVELS = 3
MEMT = 256
SCALE = HD ** -0.5
NEG = -1e30

MU, G_PRE, G_POST, G_PRE_F, G_POST_F, G_MEM, G_KV, SHIFT = 0, 6, 8, 10, 12, 14, 16, 17
W0, A0, K_K, K_A, R_K, LNX_W, LNX_B = 25, 26, 27, 28, 29, 30, 31
NVEC, NVEC_D = 32, 25

CONSTS, _at = {}, 0
for _n, _w in (("ident", 128), ("mean", 128), ("pair", 128), ("swap", 128), ("carry", T),
               ("before", C), ("upto", C), ("before_s", C), ("upto_s", C), ("level", LEVELS * C), ("level0_t", C),
               ("ids", C), ("in_batch", NB * C), ("of_batch", NB), ("eps", 1), ("lnx_eps", 1),
               ("ln_shift", 1)):
    CONSTS[_n] = (_at, _at + _w)
    _at += _w
NCONST = _at
KEYS_S = 512 + 512 + 128 + 3 * NS
KEYS_P = TP + 2 * P


SLOT = CM * T
A_R, A_K, A_V, A_A, A_LW, A_KK, A_BON, A_CL, A_TMP, A_G = [i * SLOT for i in range(10)]
A_WK = 10 * SLOT
BIG = KD * T
A_XN, A_XD, A_X1, A_X2 = A_KK, A_KK + BIG, A_KK + 2 * BIG, A_G
A_H0 = A_G
A_CAT = A_K
A_H = A_KK
HF = KF // 2
A_FH, A_FL = 0, HF * T
A_XH = 2 * HF * T
A_Y = A_H + BIG
A_XL = A_Y + BIG
A_WS = A_XL + BIG
A_U = A_WS + 8192
A_RSTD = A_U
A_SQY, A_SQH = 0, BIG
ATT = ({"cat": A_CAT, "p": 8064, "pt": 8832, "w": 256, "qs": 9600, "kt": 10112, "v": 12160},
       {"cat": 18432, "p": 20736, "pt": 36352, "w": 768, "qs": 3456, "kt": 24832, "v": 29440, "k": 34048})
A_QC, A_KC, A_VC, A_ROTK, A_ROTQ, A_COS, A_KVT = 6912, 0, 3456, 21888, A_G, 10368, 21888
A_MASKP, A_MASKC, A_MASKN, A_VCLASS, A_V0, A_VS = 10368, 5504, 13440, 14592, 16640, 17664
A_YT = 0
ARENA = A_RSTD + 2 * T
WCOL = 2048
RING = 3


def trunk(nc, I, O):

    units = []
    split_at = []
    tiles = 0

    def rows(w):
        return w.rearrange("(k p) n -> p k n", p=P)

    def add(src, nk, n, done, parts=P, split=False):
        nonlocal tiles
        tiles += done
        if split:
            split_at.append(len(units))
        units.append((src, nk, n, tiles, parts))

    def add_cols(w, c0, n, nk, step=256, split=False):
        for c in range(c0, c0 + n, step):
            add(rows(w)[:, :, c:c + step], nk, step, step // P, split=split)

    for l in range(2):
        add_cols(I["w_mem_kv"][l], 0, 512, KD)
    w_in = I["a_w_in"][0]
    add_cols(w_in, 3 * MIX, 256, KD)
    add_cols(w_in, 0, MIX, KD)
    END_R = tiles
    add(rows(I["a_w1"][0]), KD, 64, 1)
    END_W1 = tiles
    add(I["a_w2"][0].unsqueeze(1), 1, MIX, CM, 64)
    add_cols(w_in, MIX, MIX, KD)
    END_K = tiles
    add_cols(w_in, 2 * MIX, MIX, KD)
    END_V = tiles
    add(rows(I["a_a1"][0]), KD, 64, 1)
    add(I["a_a2"][0].unsqueeze(1), 1, MIX, CM, 64)
    END_A = tiles
    add(rows(I["a_g1"][0]), KD, 128, 1)
    tiles += CM
    END_KK = tiles
    add(I["a_g2"][0].unsqueeze(1), 1, MIX, CM)
    tiles += CM
    END_RK = tiles
    add_cols(I["a_w_out"][0], 0, D, KD, split=True)

    ffn_in_end = []

    def add_ffn(l):
        w1 = I["w_ffn_in"][l].rearrange("(k p) (s n) -> p k s n", p=P, s=2)
        for half in range(2):
            for u in range(half * HF, (half + 1) * HF):
                add(w1[:, :, :, u * P:(u + 1) * P], KD, 2 * P, 2, split=True)
                ffn_in_end.append(tiles)
            for c in range(0, D, P):
                add(rows(I["w_ffn_out"][l])[:, half * HF:(half + 1) * HF, c:c + P], HF, P, 1, split=True)

    add_ffn(0)
    add_cols(I["w_kv"], 0, 2 * MIX, KD, split=True)
    END_KV = tiles
    add_cols(I["b_w_in"][0], 0, D, KD, split=True)
    END_QKV = tiles
    ROT = 2 * CM
    tiles += ROT
    add_cols(I["b_w_out"][0], 0, D, 4, split=True)
    add_ffn(1)

    def landed(n):
        return 16 * sum(2 if len(units[m][0].shape) == 4 else 1 for m in range(n % RING, n + 1, RING))

    with ExitStack() as ctx:
        def sb(name, shape, dtype=F32):
            return ctx.enter_context(nc.sbuf_tensor(name, shape, dtype))

        def sem(name):
            return ctx.enter_context(nc.semaphore(name))

        banks = ctx.enter_context(nc.psum_tensor("banks", [P, 8, 512], F32))
        with nc.sbuf_tensor("arena", [P, ARENA], F32) as arena:
            pass
        cuts = sorted({0, A_FL, A_XH, A_XH + BIG, A_XL, A_WS, A_U, ARENA})
        parts_r = {a: sb(f"arena_r{a}", [P, b - a], F32R) for a, b in zip(cuts, cuts[1:])}

        def at_r(off, *dims):
            start = max(a for a in parts_r if a <= off)
            n = math.prod(dims)
            v = parts_r[start][:, off - start:off - start + n]
            return v if len(dims) == 1 else v.rearrange("p (a b) -> p a b", b=dims[-1])
        ring = sb("ring", [P, RING, WCOL])
        consts = sb("consts", [P, NCONST])
        vec = sb("vec", [P, KD, NVEC])
        mkv = sb("mkv", [P, 2, 512])
        mkt = sb("mkt", [P, 2, MEMT])
        qmem = sb("qmem", [P, 2, T])
        decay_end = sb("decay_end", [P, CM, 16])
        state = sb("state", [P, 2, CM, HD])
        small = sb("small", [P, 64])

        h_scratch = nc.dram_tensor("h_scratch", [P, BIG], F32).ap()
        mkv_scratch = nc.dram_tensor("mkv_scratch", [P, 2 * 512], F32).ap()

        def const(name):
            a, b = CONSTS[name]
            return consts[:, a:b]

        def at(off, *dims, parts=P):
            n = 1
            for d in dims:
                n *= d
            v = arena[0:parts, off:off + n]
            names = [f"d{i}" for i in range(len(dims))]
            if len(dims) == 1:
                return v
            sizes = {k: d for k, d in zip(names, dims)}
            return v.rearrange(f"p ({' '.join(names)}) -> p {' '.join(names)}", **sizes)

        ident = const("ident")
        o_centred = consts[:, CONSTS["carry"][0]:CONSTS["carry"][0] + CM * C].rearrange("p (c v) -> p c v", c=CM)

        xtok = at(0, 4, D)
        xs_tok = at(4096, D, parts=NS)
        mem_tok = at(5120, 2, D)
        mem_t = at(7168, KD, MEMT)
        mem_g = at(9216, 2, KD, MEMT)
        vrows = at(13312, D, parts=NVEC)
        mkv1 = at(14336, 2, 512)
        shift_out = at(15360, D, parts=9)
        xlast = at(16384, KD, 9)
        assert 16384 + 72 <= A_KK
        h0 = at(A_H0, KD, T)

        xn = at(A_XN, KD, T)
        xd = at(A_XD, KD, T)
        xmix = [at(A_X1, KD, T), at(A_X2, KD, T)]
        sq0 = at(A_XD, KD, T)
        lora_mid = [arena[:, A_WK + 1152 + i * T:A_WK + 1152 + (i + 1) * T] for i in range(3)]
        ln_ms = arena[:, A_RSTD:A_RSTD + T]
        rstd = arena[:, A_RSTD + T:A_RSTD + 2 * T]
        R, K, V, A, LW, KK, BON, CL, TMP, G = [at(i * SLOT, CM, T) for i in range(10)]

        h = at(A_H, KD, T)
        sq_y, sq_h, sq_f = at(A_SQY, KD, T), at(A_SQH, KD, T), at(A_XH, KD, T)
        y = at(A_Y, KD, T)
        cat = at(A_CAT, KD, T)
        x_parts = [at_r(o, KD, T) for o in (A_XH, A_XL)]
        f_parts = [at_r(o, HF, T) for o in (A_FH, A_FL)]
        w_parts = [[at_r(A_WS + (2 * i + j) * WCOL, WCOL) for j in range(2)] for i in range(2)]
        gate, up = qmem, at(A_U, 2, T)

        def flat(v):
            return v.rearrange("p a b -> p (a b)")

        zero_rows = at(16640, 512)
        def wk(i, off=A_WK):
            return at(off + i * CM * C, CM, C)

        xt_all = [at(A_LW + j * CM * C, CM, C) for j in range(NCH)]
        inv_bufs = [[wk(4 * i + n) for n in range(4)] for i in range(2)]
        prep = [[wk(n) for n in range(6)], [wk(n, A_CL) for n in range(6)]]
        u_buf, sa_buf = wk(6), wk(7)
        s0t = at(A_CL, CM, NB, HD)
        masked = at(A_CL + CM * NB * HD, CM, NB, HD)
        s0_raw = at(A_CL + CM * NB * HD, NB, CM, HD)
        o_buf = [wk(8), at(A_CL + 2 * CM * NB * HD, CM, C)]
        on_buf = [wk(9), at(A_CL + 2 * CM * NB * HD + CM * C, CM, C)]
        order = [SAMPLE] + list(range(SAMPLE))
        groups = [(0, 1), (2, 3), (4, 5), (6, 7), (SAMPLE,)]

        def levels(j):
            return SAMPLE_LEVELS if j == SAMPLE else LEVELS

        def cols(j):
            return slice(j * C, (j + 1) * C)

        def hp(i):
            return slice(HD * i, HD * i + HD)

        def over(v, n):
            return v.unsqueeze(1).broadcast_to([v.shape[0], n, v.shape[1]])

        def each(v, n):
            return v.unsqueeze(2).broadcast_to([v.shape[0], v.shape[1], n])

        def bankpair(n, m=P):
            s = n % 3
            return banks[0:m, 2 * s:2 * s + 2, 0:HALF]

        def halves(v):
            return v.rearrange("p (a b) -> p a b", a=2)

        PAIRS = NB // 2
        steps = [[("mem_p", t, hd) for t in range(4) for hd in range(4)] + [("mem_s", g, 0) for g in range(PAIRS)],
                 [("mem_p", t, hd) for t in range(4) for hd in range(4)] + [("mem_s", g, 0) for g in range(PAIRS)]
                 + [("dil_p", r, hd) for r in range(4) for hd in range(4)] + [("dil_s", g, 0) for g in range(PAIRS)]]
        ROWS = {"mem_p": P, "mem_s": 64, "dil_p": P, "dil_s": 64}
        WIDTH = {"mem_p": MEMT, "mem_s": MEMT, "dil_p": KEYS_P, "dil_s": KEYS_S}
        TURNS = {"mem_p": [[(0, 128), (128, 128)]], "mem_s": [[(0, 128), (128, 128)]],
                 "dil_p": [[(i * P, P) for i in range(4)], [(512, P), (640, P)]],
                 "dil_s": [[(i * P, P) for i in range(8)], [(1024, P), (1152, NS), (1216, NS), (1280, NS)]]}
        att = [{}, {}]
        for l in range(2):
            a, o = att[l], ATT[l]
            a["cat"] = at(o["cat"], KD if l == 0 else 4, T)
            a["mem_tile"] = CM if l == 0 else 2
            a["p"] = [at(o["p"] + i * o["w"], o["w"]) for i in range(3)]
            a["pt"] = [at(o["pt"] + i * o["w"], o["w"]) for i in range(3)]
            a["qs"] = [at(o["qs"] + i * 512, NB, 2, 4 * TS) for i in range(1 if l == 0 else 4)]
            a["kt"] = [at(o["kt"] + i * 512, 2, MEMT) for i in range(4)]
            a["kv"] = [at(o["v"] + i * 1024, 2, 512) for i in range(4)]
        kc, qc, vc = at(A_KC, CM, T), at(A_QC, CM, T), at(A_VC, CM, T)
        rot = [at(A_ROTK, CM, T), at(A_ROTQ, CM, T)]
        cos_sin = at(A_COS, 2, T)
        kv_tok = at(A_KVT, 4, 2, MIX)
        kv_new = at(A_KVT + 4 * 2 * MIX, 2, MIX, parts=NS)
        p_dil = [at(ATT[1]["p"] + i * KEYS_S, KEYS_S) for i in range(2)]
        mask_p = at(A_MASKP, 4, KEYS_P)
        mask_cached = at(A_MASKC, 1152, parts=64)
        mask_new = at(A_MASKN, PAIRS, 3 * NS, parts=64)
        v_class = at(A_VCLASS, 4, 2, 256)
        v_tok = at(A_V0, 4, 256)
        v_new = at(A_VS, 3, 256, parts=NS)
        kt_dil = [at(ATT[1]["kt"] + i * 2304, 2304) for i in range(2)]
        k_dil = [at(o, 9, 256) for o in (ATT[1]["k"], A_QC, A_QC + 2304)]
        v_dil = [at(o, 9, 256) for o in (ATT[1]["v"], ATT[1]["v"] + 2304, A_VCLASS)]
        assert A_QC + 2 * 2304 + 256 <= A_MASKN and A_VCLASS + 2304 <= A_VS
        out_rows = at(A_QC + 2 * 2304, 256, parts=64)
        KT1, KT2, KT0 = 0, 1024, 2048
        y_tok = at(A_YT, 4, D)
        y_new = at(A_YT + 4 * D, D, parts=NS)

        def stages(l):
            out, todo = [], []
            for n, (kind, _, _) in enumerate(steps[l]):
                ahead = {"mem_s": 0, "dil_s": -1}.get(kind, 1)
                done = []
                while len(todo) > max(ahead, 0):
                    done.append(todo.pop(0))
                for m in done if ahead < 0 else done[:-1]:
                    out += [("turn", m), ("values", m)]
                if kind != "dil_s" or steps[l][n - 1][0] != "dil_s":
                    out.append(("keys", n))
                if ahead < 0:
                    out.append(("scores", n))
                    if n + 1 < len(steps[l]):
                        out.append(("keys", n + 1))
                else:
                    out += [("turn", m) for m in done[-1:]] + [("scores", n)] + [("values", m) for m in done[-1:]]
                todo.append(n)
            return out + [(what, m) for m in todo for what in ("turn", "values")]

        KEY_TURNS = {"mem_s": 1, "dil_s": 5}

        def stage_turns(l, what, n):
            kind = steps[l][n][0]
            return {"keys": 2 * KEY_TURNS.get(kind, 0), "scores": 0, "turn": len(TURNS[kind]),
                    "values": 2 if kind == "dil_s" else 1}[what]

        def turns_through(l, what, n):
            order_ = stages(l)
            return (NTA if l else 0) + sum(stage_turns(l, *st) for st in order_[:order_.index((what, n)) + 1])

        NT0 = sum(stage_turns(0, *st) for st in stages(0))
        NTA = NT0 + 15 + 4
        NT1 = NTA + sum(stage_turns(1, *st) for st in stages(1))
        KV_STORES = 2 * (3 + 3)

        def first_bank(q, kind):
            return 3 * (q % 2) if kind == "dil_s" else 2 * (q % 3)

        def score_banks(q, kind):
            s = first_bank(q, kind)
            return banks[0:ROWS[kind], s:s + 3 if kind == "dil_s" else s + 2, :].rearrange("p a b -> p (a b)")[:, 0:WIDTH[kind]]

        def probs(l, q, kind):
            p = p_dil[q % 2] if kind == "dil_s" else att[l]["p"][q % 3]
            return p[0:ROWS[kind], 0:WIDTH[kind]]

        def stat(q, n, kind):
            c = 40 + 3 * n + q % 3
            return small[0:ROWS[kind], c:c + 1]

        zeroed = sem("zeroed")
        consts_in, vrows_in, x_in, xs_in, mem_in = [sem(n) for n in (
            "consts_in", "vrows_in", "x_in", "xs_in", "mem_in")]
        weights_in = [sem(f"weights_in{i}") for i in range(RING)]
        tile_ready, tile_free = sem("tile_ready"), sem("tile_free")
        vec_t, vec_ready = sem("vec_t"), sem("vec_ready")
        xt_ready, xt_free = sem("xt_ready"), sem("xt_free")
        mem_scaled, mt_ready, mt_free, mem_g_ready = [sem(n) for n in (
            "mem_scaled", "mt_ready", "mt_free", "mem_g_ready")]
        sq_ready, ms_ready, rstd_ready = [sem(n) for n in ("sq_ready", "ms_ready", "rstd_ready")]
        xn_ready, xlast_ready, xlast_t, shift_ready = [sem(n) for n in (
            "xn_ready", "xlast_ready", "xlast_t", "shift_ready")]
        mix_ready = sem("mix_ready")
        vchain, achain = sem("vector_chain"), sem("scalar_chain")
        h_ready, h_saved, h_back = sem("h_ready"), sem("h_saved"), sem("h_back")
        w_hi, w_lo, x_scaled, x_hi, x_lo = [sem(n) for n in ("w_hi", "w_lo", "x_scaled", "x_hi", "x_lo")]
        y_scaled, y_added, state_stored = sem("y_scaled"), sem("y_added"), sem("state_stored")
        kv_saved, kv_back, phase_a_stored = sem("kv_saved"), sem("kv_back"), sem("phase_a_stored")
        out_done = sem("out_done")
        mkt_t, mkt_ready = sem("mkt_t"), sem("mkt_ready")
        cat_ready = sem("cat_ready")
        u_ready, f_ready = sem("u_ready"), sem("f_ready")
        kk_ready, kk_sq, ss_clamped, kk_scale, rk_ready = [sem(n) for n in (
            "kk_ready", "kk_sq", "ss_clamped", "kk_scale", "rk_ready")]
        cum_ready, grown, shrunk, factors_ready = [sem(n) for n in (
            "cum_ready", "grown", "shrunk", "factors_ready")]
        grown_used, shifted = sem("grown_used"), sem("shifted")
        inv_l, inv_lsb, inv_y, inv_ysb, inv_t, inv_tsb, inv_d, inv_x = [sem(n) for n in (
            "inv_l", "inv_lsb", "inv_y", "inv_ysb", "inv_t", "inv_tsb", "inv_d", "inv_x")]
        s0_in, s0_t, s0_ready = sem("s0_in"), sem("s0_t"), sem("s0_ready")
        masked_ready = sem("masked_ready")
        turned, turned_out = sem("turned"), sem("turned_out")
        intra, intra_out = sem("intra"), sem("intra_out")
        u_psum, u_sb, sa_psum, sa_sb, o_psum, o_sb, ds_psum, s_new, on_ready = [sem(n) for n in (
            "u_psum", "u_sb", "sa_psum", "sa_sb", "o_psum", "o_sb", "ds_psum", "s_new", "on_ready")]
        dsm_psum, dsm_free, s0_scaled = sem("dsm_psum"), sem("dsm_free"), sem("s0_scaled")
        var_ready, gn_ready = sem("var_ready"), sem("gn_ready")
        st_t, st_out = sem("st_t"), sem("st_out")
        sm_s, sm_max, sm_exp, sm_p, sm_t, sm_pt = [sem(n) for n in (
            "sm_s", "sm_max", "sm_exp", "sm_p", "sm_t", "sm_pt")]
        qs_ready = sem("qs_ready")
        keys_in, vals_in = [[sem(f"{n}_in{i}") for i in range(3)] for n in ("keys", "vals")]
        rows_in = [sem(f"rows_in{i}") for i in range(2)]
        cos_in, masks_in, rotated, v_copied = [sem(n) for n in ("cos_in", "masks_in", "rotated", "v_copied")]
        kv_stored = sem("kv_stored")

        block = ctx.enter_context(nc.Block())

        @block.sync
        def _(sp):
            sp.dma_start(consts[:, :], I["consts"]).then_inc(consts_in, 16)
            for src, r, n in ((I["a_mu"][0], MU, 6), (I["g_pre_mix"], G_PRE, 2), (I["g_post_mix"], G_POST, 2),
                              (I["g_pre_ffn"], G_PRE_F, 2), (I["g_post_ffn"], G_POST_F, 2), (I["g_mem"], G_MEM, 2),
                              (I["g_kv"].unsqueeze(0), G_KV, 1), (I["state_shift"][0], SHIFT, NB)):
                sp.dma_start(vrows[r:r + n, :], src).then_inc(vrows_in, 16)
            for src, r in ((I["a_w0"], W0), (I["a_a0"], A0), (I["a_k_k"], K_K), (I["a_k_a"], K_A),
                           (I["a_r_k"].rearrange("a h d -> a (h d)"), R_K), (I["a_lnx_w"], LNX_W),
                           (I["a_lnx_b"], LNX_B)):
                sp.dma_start(vrows[r:r + 1, 0:MIX], src).then_inc(vrows_in, 16)
            sp.dma_start(mem_tok, I["mem_prompt"][0].rearrange("(m p) d -> p m d", p=P)).then_inc(mem_in, 16)
            sp.dma_start(xtok, I["x_prompt"][0].rearrange("(m p) d -> p m d", p=P)).then_inc(x_in, 16)
            sp.dma_start(xs_tok, I["x_sample"].rearrange("b t d -> (b t) d")).then_inc(xs_in, 16)
            def memory_rows(l):
                first = [k for k, _, _ in steps[l]].index("mem_s")
                for g in range(PAIRS):
                    if g >= 2:
                        sp.wait_ge(sm_t, turns_through(l, "values", first + g - 2))
                    for i in range(2):
                        sp.dma_start(att[l]["kv"][2 * (g % 2) + i],
                                     I["cache_mem"][l, 2 * g + i].rearrange("(m p) k h d -> p m (k h d)", p=P)).then_inc(rows_in[g % 2], 16)

            def layer0_inputs():
                sp.wait_ge(factors_ready, 1)
                states = I["state_wkv"][0].rearrange("b (c h) v k -> (h v) b c k", h=2)
                for c in range(CM):
                    sp.dma_start(s0_raw[:, :, c, :], states[:, :, c, :]).then_inc(s0_in, 16)
                sp.wait_ge(st_t, CM + 1)
                sp.wait_ge(cat_ready, 1)
                sp.wait_ge(h_saved, 16)
                sp.dma_start(flat(h), h_scratch).then_inc(h_back, 16)
                memory_rows(0)

            def layer1_inputs():
                sp.wait_ge(sm_pt, NT0)
                sp.wait_ge(phase_a_stored, 16 * 5)
                sp.dma_start(mkv[:, :, :].rearrange("p a b -> p (a b)"), mkv_scratch).then_inc(kv_back, 16)
                sp.wait_ge(h_ready, 2 * KD)
                sp.dma_start(cos_sin, I["cos_sin"]).then_inc(cos_in, 16)

            def attention_inputs():
                sp.wait_ge(rotated, 2)
                sp.dma_start(mask_p, I["mask_p"]).then_inc(masks_in, 16)
                sp.wait_ge(sm_pt, NTA)
                sp.dma_start(mask_cached, I["mask_cached"]).then_inc(masks_in, 16)
                sp.dma_start(mask_new, I["mask_new"]).then_inc(masks_in, 16)
                sp.wait_ge(v_copied, 1)
                sp.wait_ge(kv_stored, KV_STORES * 16)
                memory_rows(1)
                kinds = [k for k, _, _ in steps[1]]
                n0 = kinds.index("dil_s")
                last = len(kinds) - 1 - kinds[::-1].index("mem_s")
                sp.wait_ge(sm_t, turns_through(1, "values", last))
                for b in range(NB):
                    for kv, dst, landed_in in ((0, k_dil, keys_in), (1, v_dil, vals_in)):
                        if b >= 3 and kv == 0:
                            sp.wait_ge(sm_t, turns_through(1, "keys", n0 + (b - 3) // 2) - (0 if b % 2 == 0 else KEY_TURNS["dil_s"]))
                        elif b >= 3:
                            sp.wait_ge(sm_t, turns_through(1, "values", n0 + (b - 3) // 2))
                        elif b == 1:
                            sp.wait_ge(sm_t, turns_through(1, "values", n0 - 1))
                        dst, s = dst[b % 3], landed_in[b % 3]
                        sp.dma_start(dst[:, 0:4, :], I["cache_win_g1"][b, :, kv].rearrange("(m p) h d -> p m (h d)", p=P)).then_inc(s, 16)
                        for m in range(4):
                            rows16 = I["cache_win_g2"][b, m * 256:(m + 1) * 256, kv].rearrange("(j r) h d -> j r (h d)", r=16)
                            sp.dma_start(dst[:, 4 + m, :], rows16[:, 0:TS, :]).then_inc(s, 16)
                        sp.dma_start(dst[:, 8, :], I["cache_win_g0"][b, :, kv].rearrange("p h d -> p (h d)")).then_inc(s, 16)
                sp.wait_ge(x_lo, 4 * KD + 4)
                sp.wait_ge(h_saved, 32)
                sp.dma_start(flat(h), h_scratch).then_inc(h_back, 16)

            between = {split_at[3]: layer0_inputs, split_at[4 + 38]: layer1_inputs,
                       split_at[4 + 38 + 10 + 3]: attention_inputs}
            for n, (src, nk, w, _, parts) in enumerate(units):
                if n in between:
                    between[n]()
                if n >= RING:
                    if n - RING in split_at:
                        sp.wait_ge(w_lo, split_at.index(n - RING) + 1)
                    else:
                        sp.wait_ge(tile_ready, units[n - RING][3])
                dst = ring[0:parts, n % RING, 0:nk * w].rearrange("p (k n) -> p k n", k=nk)
                if len(src.shape) == 4:
                    for i in range(2):
                        sp.dma_start(dst[:, :, i * P:(i + 1) * P], src[:, :, i, :]).then_inc(weights_in[n % RING], 16)
                else:
                    sp.dma_start(dst, src).then_inc(weights_in[n % RING], 16)

        @block.gpsimd
        def _(pool):
            stores = [0]

            def store(dst, src):
                stores[0] += 1
                pool.dma_start(dst, src).then_inc(out_done, 16)

            nc.gpsimd.memset(zero_rows, 0.0).then_inc(zeroed, 1)
            pool.wait_ge(zeroed, 1)
            pool.dma_start(O[6][0, 0:TP].rearrange("(p r) k h d -> p (r k h d)", p=P).rearrange("p (n z) -> p n z", z=512),
                           over(zero_rows, 4)).then_inc(phase_a_stored, 16)
            pool.wait_ge(xt_free, KD + 1)
            pool.dma_start(h_scratch, flat(h0)).then_inc(h_saved, 16)
            pool.wait_ge(tile_free, 4)
            store(O[7][0, 0].rearrange("(m p) k h d -> p m (k h d)", p=P), mkv[:, :, :])
            pool.wait_ge(tile_free, 8)
            pool.dma_start(O[7][1, 0].rearrange("(m p) k h d -> p m (k h d)", p=P), mkv1).then_inc(phase_a_stored, 16)
            pool.dma_start(mkv_scratch, flat(mkv1)).then_inc(phase_a_stored, 16)
            pool.wait_ge(shift_ready, 1)
            pool.dma_start(O[3][0], shift_out[0:1, :]).then_inc(phase_a_stored, 16)
            pool.dma_start(O[9][0], shift_out[1:9, :]).then_inc(phase_a_stored, 16)
            pool.wait_ge(factors_ready, 1)
            for name, o in (("cache_win_g0", 10), ("cache_win_g1", 11), ("cache_win_g2", 12)):
                L = I[name].shape[1]
                store(O[o][:, 0:L - TS].rearrange("b l k h d -> b (l k h d)"),
                      I[name][:, TS:L].rearrange("b l k h d -> b (l k h d)"))
            pool.wait_ge(st_out, CM)
            for c in range(CM):
                store(O[8][0].rearrange("b (c h) v k -> (h v) b c k", h=2)[:, :, c, :], s0_raw[:, :, c, :])
            pool.wait_ge(st_out, CM + 1)
            pool.dma_start(O[2][0, 0].rearrange("(c h) v k -> (h v) c k", h=2), prep[0][0]).then_inc(state_stored, 16)
            pool.wait_ge(h_ready, 2 * KD)
            pool.dma_start(h_scratch, flat(h)).then_inc(h_saved, 16)
            pool.wait_ge(sm_pt, NT0 + 15)
            def store_kv(dst, src):
                pool.dma_start(dst, src).then_inc(kv_stored, 16)

            for k in range(2):
                store_kv(O[4][0, :, k].rearrange("p h d -> p (h d)"), kv_tok[:, 3, k, 0:256])
                store_kv(O[5][0, :, k].rearrange("(m p) h d -> p m (h d)", p=P), kv_tok[:, :, k, 256:512])
                store_kv(O[6][0, TP:, k].rearrange("(m p) h d -> p m (h d)", p=P), kv_tok[:, :, k, 512:768])
                for g in range(3):
                    L = I[f"cache_win_g{g}"].shape[1]
                    store_kv(O[10 + g][:, L - TS:L, k].rearrange("b t h d -> b t (h d)"), kv_new[:, k, g * 256:(g + 1) * 256])
            for m in range(TP // P):
                pool.wait_ge(sm_pt, NT1 + 2 * (m + 1))
                store(O[0][0, m * P:(m + 1) * P, :], y_tok[:, m, :])
            pool.wait_ge(sm_pt, NT1 + 10)
            store(O[1].rearrange("b t d -> (b t) d"), y_new)
            pool.wait_ge(out_done, 16 * stores[0])

        @block.tensor
        def _(pe):
            mm = nc.tensor.matmul
            tile = [0]
            unit = [0]

            def take():
                n = unit[0]
                unit[0] += 1
                _, nk, w, _, parts = units[n]
                pe.wait_ge(weights_in[n % RING], landed(n))
                return ring[0:parts, n % RING, 0:nk * w].rearrange("p (k n) -> p k n", k=nk)

            def next_tile():
                n = tile[0]
                tile[0] += 1
                if n >= 3:
                    pe.wait_ge(tile_free, n - 2)
                return 2 * (n % 3)

            def project(w, c0, m, x, nk, parts=P):
                s = next_tile()
                for k in range(nk):
                    for a in range(2):
                        last = mm(banks[0:m, s + a, 0:HALF], w[0:parts, k, c0:c0 + m],
                                  x[0:parts, k, a * HALF:(a + 1) * HALF], start=(k == 0), stop=(k == nk - 1))
                last.then_inc(tile_ready, 1)

            def project_cols(x, n, nk, step=256):
                for _ in range(n // step):
                    w = take()
                    for c in range(0, step, P):
                        project(w, c, P, x, nk)

            def mean_square(n, src, k):
                pe.wait_ge(sq_ready, KD * n + k + 1)
                for a in range(2):
                    last = mm(banks[:, 6 + a, 0:HALF], const("mean"), src[:, k, a * HALF:(a + 1) * HALF],
                              start=(k == 0), stop=(k == KD - 1))
                if k == KD - 1:
                    last.then_inc(ms_ready, 1)

            nsplit = [0]

            def take_parts():
                s = nsplit[0]
                nsplit[0] += 1
                _, nk, w, _, _ = units[split_at[s]]
                unit[0] += 1
                pe.wait_ge(w_lo, s + 1)
                return [w_parts[s % 2][j][:, 0:nk * w].rearrange("p (k n) -> p k n", k=nk) for j in range(2)]

            def project_parts(w, c0, x, nk, new_x=None, new_f=None):
                s = next_tile()
                for k in range(nk):
                    if new_x is not None:
                        pe.wait_ge(x_lo, new_x + k + 1)
                    if new_f is not None:
                        pe.wait_ge(f_ready, new_f + k + 1)
                    for m, (i, j) in enumerate(((0, 0), (1, 0), (0, 1))):
                        for a in range(2):
                            last = mm(banks[:, s + a, 0:HALF], w[i][:, k, c0:c0 + P], x[j][:, k, a * HALF:(a + 1) * HALF],
                                      start=(k == 0 and m == 0), stop=(k == nk - 1 and m == 2))
                last.then_inc(tile_ready, 1)

            def mix_out(norm, nk, new_x):
                for c in range(KD):
                    if c % 2 == 0:
                        w = take_parts()
                    project_parts(w, (c % 2) * P, x_parts, nk, new_x if c == 0 else None)
                    if c >= 2:
                        mean_square(norm, sq_y, c - 2)
                for c in range(KD - 2, KD):
                    mean_square(norm, sq_y, c)

            pe.wait_ge(consts_in, 16)
            pe.wait_ge(vrows_in, 16 * 15)
            for k in range(KD):
                n = NVEC if k < CM else NVEC_D
                last = nc.tensor.transpose(banks[:, 6, k * NVEC:k * NVEC + n], vrows[0:n, k * P:(k + 1) * P], ident[0:n, 0:n])
            last.then_inc(vec_t, 1)
            for q in range(4):
                pe.wait_ge(mem_scaled, 2)
                for k in range(2 * q, 2 * q + 2):
                    for m in range(2):
                        last = nc.tensor.transpose(banks[:, q, (k % 2) * 256 + m * P:(k % 2) * 256 + (m + 1) * P],
                                                   mem_tok[:, m, k * P:(k + 1) * P], ident)
                last.then_inc(mt_ready, 1)
            pe.wait_ge(x_in, 16)
            for k in range(KD):
                if k >= 2:
                    pe.wait_ge(xt_free, k - 1)
                for m in range(4):
                    last = nc.tensor.transpose(banks[:, 4 + k % 2, m * P:(m + 1) * P], xtok[:, m, k * P:(k + 1) * P], ident)
                last.then_inc(xt_ready, 1)
            pe.wait_ge(xs_in, 16)
            for k in range(KD):
                last = nc.tensor.transpose(banks[:, 7, k * NS:(k + 1) * NS], xs_tok[:, k * P:(k + 1) * P], ident[0:NS, 0:NS])
            last.then_inc(xt_ready, 1)
            pe.wait_ge(mt_free, 4)
            pe.wait_ge(xt_free, KD)
            for l in range(2):
                pe.wait_ge(mem_g_ready, l + 1)
                for u in range(2):
                    w = take()
                    for m in range(2):
                        s = next_tile()
                        for k in range(KD):
                            last = mm(banks[:, s, 0:256], mem_g[:, l, k, m * P:(m + 1) * P], w[:, k, :],
                                      start=(k == 0), stop=(k == KD - 1))
                        last.then_inc(tile_ready, 1)

            def turn_mem_keys(l):
                for c in range(2):
                    for m in range(2):
                        last = nc.tensor.transpose(banks[:, 6, c * 256 + m * P:c * 256 + (m + 1) * P],
                                                   mkv[:, m, c * P:(c + 1) * P], ident)
                last.then_inc(mkt_t, 1)
                pe.wait_ge(mkt_ready, l + 1)

            pe.wait_ge(tile_free, 4)
            pe.wait_ge(vec_ready, 1)
            turn_mem_keys(0)
            pe.wait_ge(xt_free, KD + 1)
            for k in range(KD):
                mean_square(0, sq0, k)
            pe.wait_ge(xn_ready, 1)
            project_cols(xn, 256, KD)
            pe.wait_ge(xlast_ready, 1)
            for k in range(KD):
                last = nc.tensor.transpose(banks[0:9, 6 + k // 4, (k % 4) * P:(k % 4 + 1) * P], xlast[:, k, :], ident)
            last.then_inc(xlast_t, 1)
            mids = iter(lora_mid)
            for i in range(6):
                pe.wait_ge(mix_ready, i + 1)
                if i in (1, 4, 5):
                    m = P if i == 5 else 64
                    project(take(), 0, m, xmix[i % 2], KD)
                    w = take()
                    mid = next(mids)
                    pe.wait_ge(tile_free, tile[0])
                    if i == 5:
                        pe.wait_ge(kk_sq, 1)
                        for c in range(CM):
                            project(const("pair").unsqueeze(1), 0, P, TMP[:, c:c + 1, :], 1)
                    for c in range(CM):
                        project(w, c * P, P, mid.unsqueeze(1), 1, m)
                else:
                    project_cols(xmix[i % 2], MIX, KD)
            pe.wait_ge(rk_ready, 1)
            for c in range(CM):
                project(const("pair").unsqueeze(1), 0, P, BON[:, c:c + 1, :], 1)

            def pairs(bank, lhs, rhs):
                for c in range(CM):
                    for i in range(2):
                        last = mm(banks[hp(i), bank, c * C:(c + 1) * C], lhs(c, i), rhs(c, i), start=True, stop=True)
                return last

            def turned_head(bank, c0, src, i):
                out, one = banks[hp(i), bank, c0:c0 + HD], ident[hp(i), hp(i)]
                if i == 0:
                    return nc.tensor.transpose(out, src, one)
                return mm(out, src, one, start=True, stop=True)

            def turned_pairs(bank, src):
                for c in range(CM):
                    for i in range(2):
                        last = turned_head(bank, c * C, src(c, i), i)
                return last

            pe.wait_ge(tile_free, tile[0])
            pe.wait_ge(factors_ready, 1)
            ny = 0
            nx = 0
            for grp in groups:
                for i, j in enumerate(grp):
                    pairs(4 * i, lambda c, q: KK[hp(q), c, cols(j)], lambda c, q: A[hp(q), c, cols(j)])
                    pairs(4 * i + 1, lambda c, q: A[hp(q), c, cols(j)],
                          lambda c, q: KK[hp(q), c, cols(j)]).then_inc(inv_l, 1)
                for lev in range(1, levels(grp[0])):
                    for i, j in enumerate(grp):
                        nx += 1
                        pe.wait_ge(inv_x, nx)
                        pairs(4 * i, lambda c, q: inv_bufs[i][1][hp(q), c, :],
                              lambda c, q: xt_all[j][hp(q), c, :]).then_inc(inv_y, 1)
                        turned_pairs(4 * i + 1, lambda c, q: xt_all[j][hp(q), c, :]).then_inc(inv_t, 1)
                    for i, j in enumerate(grp):
                        ny += 1
                        pe.wait_ge(inv_ysb, ny)
                        pe.wait_ge(inv_tsb, ny)
                        pairs(4 * i + 2, lambda c, q: inv_bufs[i][2][hp(q), c, :],
                              lambda c, q: inv_bufs[i][3][hp(q), c, :]).then_inc(inv_d, 1)
                nx += len(grp)
            pe.wait_ge(inv_x, nx)
            pe.wait_ge(s0_in, 16 * CM)

            def turn_states(bank, src, ready, free):
                for c in range(CM):
                    if c >= 2:
                        pe.wait_ge(free, c - 1)
                    for i in range(2):
                        for b in range(NB):
                            last = turned_head(bank + c % 2, b * HD, src(b, c, i), i)
                    last.then_inc(ready, 1)

            turn_states(0, lambda b, c, i: s0_raw[hp(i), b, c, :], s0_t, s0_ready)
            pe.wait_ge(s0_ready, CM)
            nturn = [0]

            def turn(lhs):
                n = nturn[0]
                nturn[0] += 1
                if n >= 3:
                    pe.wait_ge(turned_out, n - 2)
                turned_pairs(n % 3, lhs).then_inc(turned, 1)

            def prepare(n, j):
                for x in (A, K, V):
                    turn(lambda c, q: x[hp(q), c, cols(j)])
                for m, (a, b) in enumerate(((K, KK), (A, R), (K, R))):
                    if n:
                        pe.wait_ge(intra_out, 3 * (n - 1) + m + 1)
                    pairs(3 + m, lambda c, q: a[hp(q), c, cols(j)], lambda c, q: b[hp(q), c, cols(j)]).then_inc(intra, 1)

            def group(out, terms):
                for m, (a, b) in enumerate(terms):
                    last = mm(out, a, b, start=(m == 0), stop=(m == len(terms) - 1))
                return last

            prepare(0, order[0])
            for n, j in enumerate(order):
                B_, K_, V_, Lak, Lrb, Lrk = prep[n % 2]
                sample = j == SAMPLE
                pe.wait_ge(turned_out, nturn[0])
                pe.wait_ge(intra_out, 3 * (n + 1))
                if n:
                    pe.wait_ge(s_new, n)

                def from_state(c, i, chan):
                    if sample:
                        return [(masked[hp(i), c, b, :], s0t[hp(i), c, b, :]) for b in range(NB)]
                    return [(chan[hp(i), c, cols(j)], state[hp(i), n % 2, c, :])]

                def outputs_of_chunk():
                    for c in range(CM):
                        for i in range(2):
                            last = group(banks[hp(i), 7, c * C:(c + 1) * C],
                                         from_state(c, i, R) + [(Lrb[hp(i), c, :], sa_buf[hp(i), c, :]),
                                                                (Lrk[hp(i), c, :], V_[hp(i), c, :])])
                    last.then_inc(o_psum, 1)

                if sample:
                    pe.wait_ge(masked_ready, 1)
                for c in range(CM):
                    for i in range(2):
                        last = group(banks[hp(i), 6, c * C:(c + 1) * C],
                                     from_state(c, i, KK) + [(Lak[hp(i), c, :], V_[hp(i), c, :])])
                last.then_inc(u_psum, 1)
                if n + 1 < NCH and not sample:
                    prepare(n + 1, order[n + 1])
                pe.wait_ge(u_sb, n + 1)
                if n:
                    pe.wait_ge(o_sb, n)
                pairs(7, lambda c, q: xt_all[j][hp(q), c, :], lambda c, q: u_buf[hp(q), c, :]).then_inc(sa_psum, 1)
                if n:
                    pe.wait_ge(on_ready, n)
                    turn(lambda c, q: on_buf[(n - 1) % 2][hp(q), c, :])
                pe.wait_ge(sa_sb, n + 1)
                if sample:
                    pe.wait_ge(masked_ready, 2)
                    outputs_of_chunk()
                    for q, tok in enumerate((B_, K_)):
                        pe.wait_ge(masked_ready, 3 + q)
                        for c in range(CM):
                            m = q * CM + c
                            if m >= 2:
                                pe.wait_ge(dsm_free, m - 1)
                            for i in range(2):
                                last = mm(banks[hp(i), 4 + m % 2, :], tok[hp(i), c, :],
                                          masked[hp(i), c, :, :].rearrange("p b v -> p (b v)"), start=True, stop=True)
                            last.then_inc(dsm_psum, 1)
                    pe.wait_ge(s0_scaled, 1)
                    turn_states(4, lambda b, c, i: s0t[hp(i), c, b, :], st_t, st_out)
                    pe.wait_ge(st_out, CM)
                    prepare(n + 1, order[n + 1])
                else:
                    for c in range(CM):
                        for i in range(2):
                            last = group(banks[hp(i), 6, c * C:(c + 1) * C],
                                         [(B_[hp(i), c, :], sa_buf[hp(i), c, :]), (K_[hp(i), c, :], V_[hp(i), c, :])])
                    last.then_inc(ds_psum, 1)
                    outputs_of_chunk()
            pe.wait_ge(on_ready, NCH)
            turn(lambda c, q: on_buf[(NCH - 1) % 2][hp(q), c, :])
            pe.wait_ge(s_new, NCH)
            turned_pairs(6, lambda c, q: state[hp(q), NCH % 2, c, :]).then_inc(st_t, 1)
            pe.wait_ge(turned_out, nturn[0])
            pe.wait_ge(st_out, CM + 1)

            nt = [0]
            nq = [0]

            def turn_blocks(blocks):
                n = nt[0]
                nt[0] += 1
                if n >= 2:
                    pe.wait_ge(sm_pt, n - 1)
                for src, c0 in blocks:
                    m, w = src.shape[0], src.shape[1]
                    last = nc.tensor.transpose(banks[0:w, 6 + n % 2, c0:c0 + m], src, ident[0:m, 0:m])
                last.then_inc(sm_t, 1)

            def window_keys(b):
                k = k_dil[b % 3]
                pe.wait_ge(keys_in[b % 3], 6 * 16 * (b // 3 + 1))
                for c0, tiles_ in ((0, range(0, 4)), (1, range(0, 4)), (0, range(4, 8)), (1, range(4, 8))):
                    turn_blocks([(k[:, t_, c0 * P:(c0 + 1) * P], m * P) for m, t_ in enumerate(tiles_)])
                turn_blocks([(k[:, 8, c0 * P:(c0 + 1) * P], c0 * P) for c0 in range(2)])

            nk = [0]

            def turn_keys(l, q, kind, x, hd):
                for b in range(2):
                    if kind == "mem_s":
                        rows_ = att[l]["kv"][2 * (x % 2) + b]
                        if b == 0:
                            pe.wait_ge(rows_in[x % 2], 32 * (l * PAIRS // 2 + x // 2 + 1))
                        turn_blocks([(rows_[:, m, c * P:(c + 1) * P], c * MEMT + m * P) for c in range(2) for m in range(2)])
                    elif kind == "dil_s":
                        window_keys(2 * x + b)
                nk[0] = nt[0]

            def scores(l, q, kind, x, hd):
                a = att[l]
                s = first_bank(q, kind)
                c, i = hd // 2, hd % 2
                if kind == "dil_s":
                    pe.wait_ge(sm_exp, q)
                elif q >= 3:
                    pe.wait_ge(sm_exp, q - 2)
                if kind == "mem_p":
                    last = mm(banks[:, s, 0:MEMT], qmem[hp(i), c, x * P:(x + 1) * P], mkt[hp(i), c, :], start=True, stop=True)
                elif kind == "dil_p":
                    tok = slice(x, TP, 4)
                    mm(banks[:, s, 0:TP], qc[hp(i), c, tok], kc[hp(i), c, 0:TP], start=True, stop=True)
                    for g in (1, 2):
                        last = mm(banks[:, s + 1, (g - 1) * P:g * P], qc[hp(i), 2 * g + c, tok], kc[hp(i), 2 * g + c, tok],
                                  start=True, stop=True)
                elif kind == "mem_s":
                    pe.wait_ge(sm_pt, nk[0])
                    for b in range(2):
                        last = group(banks[32 * b:32 * b + 32, s, 0:MEMT],
                                     [(a["qs"][0][:, 2 * x + b, c, :], a["kt"][2 * (x % 2) + b][:, c, :]) for c in range(2)])
                else:
                    pe.wait_ge(sm_pt, nk[0])
                    for b in range(2):
                        def part(bank, c0, n, g, keys):
                            return group(banks[32 * b:32 * b + 32, s + bank, c0:c0 + n],
                                         [(a["qs"][1 + g][:, 2 * x + b, c, :], keys(c)) for c in range(2)])
                        part(0, 0, 512, 1, lambda c: kt_dil[b][:, KT1 + c * 512:KT1 + (c + 1) * 512])
                        part(1, 0, 512, 2, lambda c: kt_dil[b][:, KT2 + c * 512:KT2 + (c + 1) * 512])
                        part(2, 0, P, 0, lambda c: kt_dil[b][:, KT0 + c * P:KT0 + (c + 1) * P])
                        for g in range(3):
                            last = part(2, P + g * NS, NS, g, lambda c: kc[:, 2 * g + c, TP:T])
                last.then_inc(sm_s, 1)

            def turn_probs(l, q, kind, x, hd):
                rows = ROWS[kind]
                pe.wait_ge(sm_p, q + 1)
                for blocks in TURNS[kind]:
                    turn_blocks([(probs(l, q, kind)[:, k0:k0 + w], m * rows) for m, (k0, w) in enumerate(blocks)])

            def weigh(l, q, kind, x, hd):
                a = att[l]
                rows = ROWS[kind]
                c, i = hd // 2, hd % 2
                pe.wait_ge(sm_pt, nt[0])
                s = 6 + nt[0] % 2
                nt[0] += 1
                pt = a["pt"][q % 3]

                def ptb(m, w=P):
                    return pt[0:w, m * rows:(m + 1) * rows]

                if kind == "mem_p":
                    last = group(banks[hp(i), s, 0:P], [(mkv[:, m, 256 + hd * HD:256 + (hd + 1) * HD], ptb(m)) for m in range(2)])
                elif kind == "dil_p":
                    hc = slice(hd * HD, (hd + 1) * HD)
                    last = group(banks[hp(i), s, 0:P], [(v_tok[:, m, hc], ptb(m)) for m in range(4)]
                                 + [(v_class[:, x, g, hc], ptb(4 + g)) for g in range(2)])
                elif kind == "mem_s":
                    for b in range(2):
                        for c in range(2):
                            q0 = 32 * b + 16 * c
                            last = group(banks[:, s, q0:q0 + 16],
                                         [(a["kv"][2 * (x % 2) + b][:, m, 256 + c * P:256 + (c + 1) * P],
                                           ptb(m)[:, q0:q0 + 16]) for m in range(2)])
                else:
                    for b in range(2):
                        n = 2 * x + b
                        pe.wait_ge(vals_in[n % 3], 6 * 16 * (n // 3 + 1))
                        rb = slice(32 * b, 32 * b + 32)
                        last = group(banks[rb, s, 0:256], [(ptb(m)[:, rb], v_dil[n % 3][:, m, :]) for m in range(9)]
                                     + [(ptb(9 + g, NS)[:, rb], v_new[:, g, :]) for g in range(3)])
                last.then_inc(sm_t, 1)
                if kind == "dil_s":
                    pe.wait_ge(sm_pt, nt[0])
                    turn_blocks([(out_rows[:, c * P:(c + 1) * P], c * 64) for c in range(2)])

            def attention(l, q0):
                stage = {"keys": turn_keys, "scores": scores, "turn": turn_probs, "values": weigh}
                for what, n in stages(l):
                    stage[what](l, q0 + n, *steps[l][n])
                pe.wait_ge(sm_pt, nt[0])

            pe.wait_ge(qs_ready, 1)
            attention(0, 0)
            mix_out(1, KD, 0)

            def feed_forward(l, norm, new_x):
                for k in range(KD):
                    mean_square(norm + 1, sq_h, k)
                for half in range(2):
                    for u in range(HF):
                        w = take_parts()
                        for c in range(2):
                            project_parts(w, c * P, x_parts, KD, new_x if half == u == c == 0 else None)
                    for c in range(KD):
                        project_parts(take_parts(), 0, f_parts, HF, new_f=None if c else KF * l + half * HF)
                        if half and c >= 2:
                            mean_square(norm + 2, sq_f, c - 2)
                for c in range(KD - 2, KD):
                    mean_square(norm + 2, sq_f, c)

            feed_forward(0, 1, KD)
            pe.wait_ge(kv_back, 16)
            pe.wait_ge(rstd_ready, 4)
            turn_mem_keys(1)
            for k in range(KD):
                mean_square(4, sq_h, k)
            for n, new_x in ((2 * MIX, 2 * KD), (D, 3 * KD)):
                for c in range(n // P):
                    if c % 2 == 0:
                        w = take_parts()
                    project_parts(w, (c % 2) * P, x_parts, KD, new_x if c == 0 else None)
            pe.wait_ge(tile_free, END_QKV)
            for x in (kc, qc):
                for c in range(CM):
                    project(const("swap").unsqueeze(1), 0, P, x[:, c:c + 1, :], 1)
            pe.wait_ge(rotated, 1)
            for m in range(5):
                tok = slice(m * P, (m + 1) * P) if m < 4 else slice(TP, T)
                rows_ = [x[:, c, tok] for x in (kc, vc) for c in range(CM)]
                for q in range(3):
                    turn_blocks([(r, n * P) for n, r in enumerate(rows_[4 * q:4 * q + 4])])
            for r in range(4):
                turn_blocks([(vc[:, CM // 3 + n, slice(r, TP, 4)], n * P) for n in range(4)])
            pe.wait_ge(qs_ready, 2)
            pe.wait_ge(v_copied, 1)
            attention(1, len(steps[0]))
            mix_out(5, 4, 4 * KD)
            feed_forward(1, 5, 4 * KD + 4)
            pe.wait_ge(h_ready, 4 * KD)
            for k in range(4):
                for q in range(2):
                    turn_blocks([(h[:, 4 * q + n, k * P:(k + 1) * P], n * P) for n in range(4)])
            for q in range(2):
                turn_blocks([(h[:, 4 * q + n, TP:T], n * P) for n in range(4)])

        @block.scalar
        def _(act):
            f = nc.scalar.activation
            tile = [0]
            chain = [0]

            def link(ins):
                chain[0] += 1
                ins.then_inc(achain, 1)
                act.wait_ge(achain, chain[0])

            def drain_tile(out, func, m=P, **kw):
                n = tile[0]
                tile[0] += 1
                act.wait_ge(tile_ready, n + 1)
                f(halves(out), bankpair(n, m), func, **kw).then_inc(tile_free, 1)

            def square(dst, src, k):
                f(dst[:, k, :], src[:, k, :], ACT.Square).then_inc(sq_ready, 1)

            def norm_scale(n):
                act.wait_ge(ms_ready, n + 1)
                link(f(halves(ln_ms), banks[:, 6:8, 0:HALF], ACT.Ln, bias=const("eps")))
                f(rstd, ln_ms, ACT.Exp, scale=-0.5).then_inc(rstd_ready, 1)

            act.wait_ge(consts_in, 16)
            act.wait_ge(mem_in, 16)
            for m in range(2):
                last = f(at(A_XN + m * D, D), mem_tok[:, m, :], ACT.Square, accum_out=small[:, m:m + 1])
            link(last)
            link(f(small[:, 2:4], small[:, 0:2], ACT.Ln, bias=const("eps"), scale=1.0 / D))
            link(f(small[:, 4:6], small[:, 2:4], ACT.Exp, scale=-0.5))
            for m in range(2):
                f(mem_tok[:, m, :], mem_tok[:, m, :], ACT.Copy, scale=small[:, 4 + m:5 + m]).then_inc(mem_scaled, 1)
            act.wait_ge(vec_t, 1)
            f(vec[:, 0:CM, :], banks[:, 6, 0:CM * NVEC].rearrange("p (k n) -> p k n", k=CM), ACT.Copy)
            f(vec[:, CM:KD, 0:NVEC_D], banks[:, 6, CM * NVEC:KD * NVEC].rearrange("p (k n) -> p k n", n=NVEC)[:, :, 0:NVEC_D],
              ACT.Copy).then_inc(vec_ready, 1)
            for q in range(4):
                act.wait_ge(mt_ready, q + 1)
                f(flat(mem_t[:, 2 * q:2 * q + 2, :]), banks[:, q, :], ACT.Copy).then_inc(mt_free, 1)
            for k in range(KD):
                act.wait_ge(xt_ready, k + 1)
                f(h0[:, k, 0:TP], banks[:, 4 + k % 2, :], ACT.Copy).then_inc(xt_free, 1)
            act.wait_ge(xt_ready, KD + 1)
            f(h0[:, :, TP:T], banks[:, 7, :].rearrange("p (k n) -> p k n", k=KD), ACT.Copy).then_inc(xt_free, 1)
            for l in range(2):
                for u in range(2):
                    for m in range(2):
                        n = tile[0]
                        tile[0] += 1
                        act.wait_ge(tile_ready, n + 1)
                        f((mkv[:, :, :], mkv1)[l][:, m, u * 256:(u + 1) * 256], banks[:, 2 * (n % 3), 0:256], ACT.Copy).then_inc(tile_free, 1)

            def mem_keys(l):
                act.wait_ge(mkt_t, l + 1)
                f(mkt[:, :, :].rearrange("p a b -> p (a b)"), banks[:, 6, :], ACT.Copy).then_inc(mkt_ready, 1)

            mem_keys(0)
            act.wait_ge(xt_free, KD + 1)
            for k in range(KD):
                square(sq0, h0, k)
            norm_scale(0)
            for c in range(2):
                drain_tile(qmem[:, c, :], ACT.Copy)
            act.wait_ge(xlast_t, 1)
            f(shift_out.rearrange("p (a b) -> p a b", a=2), banks[0:9, 6:8, :], ACT.Copy).then_inc(shift_ready, 1)
            for c in range(CM):
                drain_tile(R[:, c, :], ACT.Copy)
            drain_tile(lora_mid[0][0:64, :], ACT.Tanh, m=64)
            act.wait_ge(phase_a_stored, 16 * 5)
            for c in range(CM):
                drain_tile(LW[:, c, :], ACT.Sigmoid, bias=vec[:, c, W0:W0 + 1])
            for buf in (K, V):
                for c in range(CM):
                    drain_tile(buf[:, c, :], ACT.Copy)
            drain_tile(lora_mid[1][0:64, :], ACT.Copy, m=64)
            for c in range(CM):
                drain_tile(A[:, c, :], ACT.Sigmoid, bias=vec[:, c, A0:A0 + 1])
            drain_tile(lora_mid[2], ACT.Sigmoid)
            act.wait_ge(kk_ready, 1)
            f(flat(TMP), flat(KK), ACT.Square).then_inc(kk_sq, 1)
            for c in range(CM):
                drain_tile(CL[:, c, :], ACT.Copy)
            for c in range(CM):
                drain_tile(G[:, c, :], ACT.Copy)
            act.wait_ge(ss_clamped, 1)
            link(f(flat(TMP), flat(CL), ACT.Ln, scale=2.0 ** 20))
            f(flat(CL), flat(TMP), ACT.Exp, scale=-0.5, bias=const("ln_shift")).then_inc(kk_scale, 1)
            act.wait_ge(kk_scale, 1)
            for c in range(CM):
                drain_tile(TMP[:, c, :], ACT.Copy)
            act.wait_ge(cum_ready, 1)
            f(flat(TMP), flat(CL), ACT.Exp).then_inc(grown, 1)
            act.wait_ge(shifted, 1)
            f(flat(LW), flat(LW), ACT.Exp).then_inc(grown, 1)
            act.wait_ge(grown_used, 1)
            f(flat(TMP), flat(CL), ACT.Exp, scale=-1.0).then_inc(shrunk, 1)

            nl = ny = 0
            for grp in groups:
                for i, j in enumerate(grp):
                    nl += 1
                    act.wait_ge(inv_l, nl)
                    f(flat(inv_bufs[i][0]), banks[:, 4 * i, 0:CM * C], ACT.Copy).then_inc(inv_lsb, 1)
                for lev in range(1, levels(grp[0])):
                    for i, j in enumerate(grp):
                        ny += 1
                        act.wait_ge(inv_y, ny)
                        f(flat(inv_bufs[i][3]), banks[:, 4 * i, 0:CM * C], ACT.Copy).then_inc(inv_ysb, 1)
                        act.wait_ge(inv_t, ny)
                        f(flat(inv_bufs[i][2]), banks[:, 4 * i + 1, 0:CM * C], ACT.Copy).then_inc(inv_tsb, 1)
            for c in range(CM):
                act.wait_ge(s0_t, c + 1)
                f(s0t[:, c, :, :].rearrange("p b v -> p (b v)"), banks[:, c % 2, :], ACT.Copy).then_inc(s0_ready, 1)
            nturn = [0]

            def turned_to(dst, to_chunk=None):
                n = nturn[0]
                nturn[0] += 1
                act.wait_ge(turned, n + 1)
                f(dst, banks[:, n % 3, 0:CM * C].rearrange("p (c v) -> p c v", c=CM), ACT.Copy).then_inc(turned_out, 1)

            def prepare(n):
                for m in range(3):
                    turned_to(prep[n % 2][m])

            prepare(0)
            for n, j in enumerate(order):
                act.wait_ge(u_psum, n + 1)
                f(flat(u_buf), banks[:, 6, 0:CM * C], ACT.Copy).then_inc(u_sb, 1)
                if n:
                    act.wait_ge(var_ready, n)
                    link(f(small[:, 24:30], small[:, 18:24], ACT.Ln, scale=1.0 / HD, bias=const("lnx_eps")))
                    f(small[:, 30:36], small[:, 24:30], ACT.Exp, scale=-0.5).then_inc(gn_ready, 1)
                    if n + 1 < NCH:
                        prepare(n + 1)
                act.wait_ge(sa_psum, n + 1)
                f(flat(sa_buf), banks[:, 7, 0:CM * C], ACT.Copy).then_inc(sa_sb, 1)
                if n:
                    turned_to(R[:, :, cols(order[n - 1])])
                if n >= 2:
                    act.wait_ge(on_ready, n - 1)
                act.wait_ge(o_psum, n + 1)
                f(flat(o_buf[n % 2]), banks[:, 7, 0:CM * C], ACT.Copy).then_inc(o_sb, 1)
                if not n:
                    for c in range(CM):
                        act.wait_ge(st_t, c + 1)
                        f(s0_raw[:, :, c, :], banks[:, 4 + c % 2, :].rearrange("p (b k) -> p b k", b=NB), ACT.Copy).then_inc(st_out, 1)
                    prepare(1)
            act.wait_ge(var_ready, NCH)
            link(f(small[:, 24:30], small[:, 18:24], ACT.Ln, scale=1.0 / HD, bias=const("lnx_eps")))
            f(small[:, 30:36], small[:, 24:30], ACT.Exp, scale=-0.5).then_inc(gn_ready, 1)
            turned_to(R[:, :, cols(order[-1])])
            act.wait_ge(st_t, CM + 1)
            f(flat(prep[0][0]), banks[:, 6, 0:CM * C], ACT.Copy).then_inc(st_out, 1)

            nt = [0]

            def turned_blocks(dst, c0, n, m=P, **kw):
                b = nt[0]
                nt[0] += 1
                act.wait_ge(sm_t, b + 1)
                src = banks[0:m, 6 + b % 2, c0:c0 + n]
                return f(dst, src, ACT.Copy).then_inc(sm_pt, 1)

            def exps(l, q, kind, x, hd):
                act.wait_ge(sm_max, q + 1)
                f(probs(l, q, kind), score_banks(q, kind), ACT.Exp, scale=SCALE, bias=stat(q, 0, kind),
                  accum_out=stat(q, 1, kind)).then_inc(sm_exp, 1)

            pending = []

            def exps_due():
                if pending:
                    exps(*pending.pop())

            def keys(l, kind, x):
                for b in range(2):
                    if kind == "mem_s":
                        turned_blocks(flat(att[l]["kt"][2 * (x % 2) + b]), 0, 512)
                    elif kind == "dil_s":
                        for k0 in (KT1, KT1 + 512, KT2, KT2 + 512):
                            turned_blocks(kt_dil[b][:, k0:k0 + 512], 0, 512)
                        turned_blocks(kt_dil[b][:, KT0:KT0 + 256], 0, 256)
                        exps_due()

            def probs_out(l, q, kind):
                rows = ROWS[kind]
                pt = att[l]["pt"][q % 3]
                at_ = 0
                for blocks in TURNS[kind]:
                    full = [b for b in blocks if b[1] == P]
                    part = len(blocks) - len(full)
                    w = len(full) * rows
                    if not part:
                        turned_blocks(pt[:, at_:at_ + w], 0, w)
                    else:
                        b = nt[0]
                        nt[0] += 1
                        act.wait_ge(sm_t, b + 1)
                        f(pt[:, at_:at_ + w], banks[:, 6 + b % 2, 0:w], ACT.Copy)
                        f(pt[0:NS, at_ + w:at_ + w + part * rows], banks[0:NS, 6 + b % 2, w:w + part * rows],
                          ACT.Copy).then_inc(sm_pt, 1)
                    at_ += len(blocks) * rows

            def attention(l, q0):
                for what, n in stages(l):
                    kind, x, hd = steps[l][n]
                    if what == "keys":
                        keys(l, kind, x)
                    elif what == "scores":
                        exps_due()
                        pending.append((l, q0 + n, kind, x, hd))
                    elif what == "turn":
                        if pending and pending[0][1] == q0 + n:
                            exps_due()
                        probs_out(l, q0 + n, kind)
                    else:
                        gather(l, kind, x, hd)
                        exps_due()

            def gather(l, kind, x, hd):
                a = att[l]
                if kind == "dil_s":
                    turned_blocks(out_rows, 0, 256, m=64)
                c, i = hd // 2, hd % 2
                b = nt[0]
                nt[0] += 1
                act.wait_ge(sm_t, b + 1)
                src = banks[:, 6 + b % 2, :]
                if kind == "mem_p":
                    last = f(a["cat"][hp(i), a["mem_tile"] + c, x * P:(x + 1) * P], src[hp(i), 0:P], ACT.Copy)
                elif kind == "dil_p":
                    last = f(a["cat"][hp(i), c, slice(x, TP, 4)], src[hp(i), 0:P], ACT.Copy)
                else:
                    c0 = a["mem_tile"] if kind == "mem_s" else 0
                    for c in range(2):
                        for i in range(2):
                            first = 64 * c if kind == "dil_s" else 0
                            last = f(a["cat"][hp(i), c0 + c, TP + 16 * x:TP + 16 * x + 16].rearrange("p (b t) -> p b t", b=2),
                                     src[hp(i), first:first + 64].rearrange("p (b c i t) -> p b c i t", b=2, c=2, i=2)[:, :, c, i, :],
                                     ACT.Copy)
                last.then_inc(sm_pt, 1)

            attention(0, 0)

            nsplit, nx = [0], [0]

            def high_weights():
                s = nsplit[0]
                nsplit[0] += 1
                n = split_at[s]
                _, nk, w, _, _ = units[n]
                act.wait_ge(weights_in[n % RING], landed(n))
                if s >= 2:
                    act.wait_ge(tile_ready, units[split_at[s - 2]][3])
                f(w_parts[s % 2][0][:, 0:nk * w], ring[:, n % RING, 0:nk * w], ACT.Copy).then_inc(w_hi, 1)

            def high_input(src, k):
                f(x_parts[0][:, k, :], src[:, k, :], ACT.Copy).then_inc(x_hi, 1)

            def high_scaled(first):
                for k in range(KD):
                    act.wait_ge(x_scaled, first + k + 1)
                    high_input(y, k)

            def mix_out(norm, src, nk):
                high_weights()
                for k in range(nk):
                    high_input(src, k)
                for c in range(KD):
                    if c % 2 == 0 and c < KD - 2:
                        high_weights()
                    drain_tile(y[:, c, :], ACT.Copy)
                    if c:
                        act.wait_ge(tile_free, tile[0] - 1)
                        square(sq_y, y, c - 1)
                act.wait_ge(tile_free, tile[0])
                square(sq_y, y, KD - 1)
                norm_scale(norm)

            def feed_forward(l, norm):
                high_weights()
                for k in range(KD):
                    act.wait_ge(h_ready, 2 * KD * l + k + 1)
                    square(sq_h, h, k)
                norm_scale(norm + 1)
                high_scaled(KD * (3 * l))
                for half in range(2):
                    for u in range(half * HF, (half + 1) * HF):
                        high_weights()
                        m = u + KF * l
                        if u >= 2:
                            act.wait_ge(f_ready, m - 1)
                        drain_tile(gate[:, u % 2, :], ACT.Silu)
                        drain_tile(up[:, u % 2, :], ACT.Copy)
                    if half:
                        act.wait_ge(f_ready, (l + 1) * KF)
                    for c in range(KD):
                        if not (half and c == KD - 1):
                            high_weights()
                        if half and c >= 2:
                            act.wait_ge(y_added, KD * l + c - 1)
                        drain_tile(up[:, c % 2, :] if half else y[:, c, :], ACT.Copy)
                        if half and c:
                            act.wait_ge(y_added, KD * l + c)
                            square(sq_f, y, c - 1)
                act.wait_ge(y_added, KD * (l + 1))
                square(sq_f, y, KD - 1)
                norm_scale(norm + 2)

            act.wait_ge(cat_ready, 1)
            act.wait_ge(sm_pt, NT0)
            act.wait_ge(state_stored, 16)
            mix_out(1, att[0]["cat"], KD)
            feed_forward(0, 1)
            mem_keys(1)
            high_weights()
            for k in range(KD):
                act.wait_ge(h_ready, KD + k + 1)
                square(sq_h, h, k)
            norm_scale(4)
            high_scaled(KD)
            for buf in (kc, vc):
                for c in range(CM):
                    if c % 2 == 0:
                        high_weights()
                    drain_tile(buf[:, c, :], ACT.Copy)
            high_scaled(2 * KD)
            for c in range(CM):
                if c % 2 == 0:
                    high_weights()
                drain_tile(qc[:, c, :], ACT.Copy)
            for c in range(2):
                drain_tile(qmem[:, c, :], ACT.Copy)
            for buf in rot:
                for c in range(CM):
                    drain_tile(buf[:, c, :], ACT.Copy)
            for m in range(5):
                for q in range(3):
                    b = nt[0]
                    nt[0] += 1
                    act.wait_ge(sm_t, b + 1)
                    if m < 4:
                        dst = kv_tok[:, m, :, :].rearrange("p k n -> p (k n)")[:, q * 512:(q + 1) * 512]
                    else:
                        dst = kv_new.rearrange("p k n -> p (k n)")[:, q * 512:(q + 1) * 512]
                    f(dst, banks[0:(P if m < 4 else NS), 6 + b % 2, :], ACT.Copy).then_inc(sm_pt, 1)
            for r in range(4):
                turned_blocks(v_class[:, r, :, :].rearrange("p g n -> p (g n)"), 0, 512)
            act.wait_ge(v_copied, 1)
            act.wait_ge(kv_stored, KV_STORES * 16)
            attention(1, len(steps[0]))
            act.wait_ge(sm_pt, NT1)
            mix_out(5, att[1]["cat"], 4)
            feed_forward(1, 5)
            for k in range(4):
                for q in range(2):
                    turned_blocks(y_tok[:, k, q * 512:(q + 1) * 512], 0, 512)
            for q in range(2):
                turned_blocks(y_new[:, q * 512:(q + 1) * 512], 0, 512, m=NS)

        @block.vector
        def _(dve):
            v = nc.vector
            chain = [0]

            def link(ins):
                chain[0] += 1
                ins.then_inc(vchain, 1)
                dve.wait_ge(vchain, chain[0])

            dve.wait_ge(consts_in, 16)
            v.memset(state[:, 1], 0.0).then_inc(s_new, 1)
            dve.wait_ge(mt_free, 4)
            dve.wait_ge(vec_ready, 1)
            for l in range(2):
                v.tensor_tensor(mem_g[:, l], mem_t, each(vec[:, :, G_MEM + l], MEMT), ALU.mult).then_inc(mem_g_ready, 1)

            def normed(dst, src, g, last_sem, n=KD):
                for k in range(n):
                    ins = v.scalar_tensor_tensor(dst[:, k, :], src[:, k, :], vec[:, k, g:g + 1], rstd, ALU.mult, ALU.mult)
                ins.then_inc(last_sem, 1)

            dve.wait_ge(rstd_ready, 1)
            normed(xn, h0, G_PRE, xn_ready)
            dve.wait_ge(xn_ready, 1)
            v.tensor_tensor(xd[:, :, 1:TP], xn[:, :, 0:TP - 1], xn[:, :, 1:TP], ALU.subtract)
            v.tensor_scalar(xd[:, :, 0:1], xn[:, :, 0:1], -1.0, None, ALU.mult)
            xns, xds = [a[:, :, TP:T].rearrange("p k (b t) -> p k b t", b=NB) for a in (xn, xd)]
            v.tensor_tensor(xds[:, :, :, 1:TS], xns[:, :, :, 0:TS - 1], xns[:, :, :, 1:TS], ALU.subtract)
            v.tensor_tensor(xds[:, :, :, 0], vec[:, :, SHIFT:SHIFT + NB], xns[:, :, :, 0], ALU.subtract)
            v.tensor_copy(xlast[:, :, 0:1], xn[:, :, TP - 1:TP])
            link(v.tensor_copy(xlast[:, :, 1:9], xns[:, :, :, TS - 1]))
            v.tensor_copy(small[:, 36:37], const("eps")).then_inc(xlast_ready, 1)
            ends = (END_R, END_W1, END_K, END_V)
            for i in range(6):
                if i >= 2:
                    dve.wait_ge(tile_ready, ends[i - 2])
                if i == 1:
                    dve.wait_ge(h_saved, 16)
                for k in range(KD):
                    ins = v.scalar_tensor_tensor(xmix[i % 2][:, k, :], xd[:, k, :], vec[:, k, MU + i:MU + i + 1],
                                                 xn[:, k, :], ALU.mult, ALU.add)
                ins.then_inc(mix_ready, 1)
            dve.wait_ge(tile_free, END_A)
            dve.wait_ge(mix_ready, 6)
            for c in range(CM):
                ins = v.tensor_scalar(KK[:, c, :], K[:, c, :], vec[:, c, K_K:K_K + 1], None, ALU.mult)
            ins.then_inc(kk_ready, 1)
            link(v.tensor_scalar(flat(LW), flat(LW), -float(2.718281828459045 ** -0.5), None, ALU.mult))
            for c in range(CM):
                ins = v.tensor_scalar(BON[:, c, :], A[:, c, :], 1.0, vec[:, c, K_A:K_A + 1], ALU.subtract, ALU.mult)
            link(ins)
            link(v.scalar_tensor_tensor(flat(K), flat(BON), 1.0, flat(K), ALU.add, ALU.mult))
            for c in range(CM):
                ins = v.scalar_tensor_tensor(BON[:, c, :], R[:, c, :], vec[:, c, R_K:R_K + 1], K[:, c, :], ALU.mult, ALU.mult)
            ins.then_inc(rk_ready, 1)
            dve.wait_ge(tile_free, END_KK)
            v.tensor_scalar(flat(CL), flat(CL), 1e-24, None, ALU.max).then_inc(ss_clamped, 1)
            dve.wait_ge(kk_scale, 1)
            link(v.tensor_tensor(flat(KK), flat(KK), flat(CL), ALU.mult))
            v.tensor_tensor(flat(A), flat(A), flat(KK), ALU.mult)
            for c in range(CM):
                ins = v.tensor_tensor_scan(CL[:, c, :], const("carry"), LW[:, c, :], 0.0, ALU.mult, ALU.add)
            link(ins)
            dve.wait_ge(tile_free, END_RK)
            link(v.tensor_tensor(flat(BON), flat(TMP), flat(V), ALU.mult))
            v.tensor_copy(small[:, 37:38], const("eps")).then_inc(cum_ready, 1)
            v.tensor_tensor(flat(LW), flat(CL), flat(LW), ALU.subtract).then_inc(shifted, 1)
            dve.wait_ge(grown, 1)
            v.tensor_copy(decay_end[:, :, 0:8], TMP[:, :, C - 1:TP:C])
            v.tensor_copy(decay_end[:, :, 8:16], TMP[:, :, TP + TS - 1:T:TS])
            v.tensor_tensor(flat(R), flat(R), flat(TMP), ALU.mult).then_inc(grown_used, 1)
            dve.wait_ge(grown, 2)
            link(v.scalar_tensor_tensor(flat(KK), flat(KK), -1.0, flat(LW), ALU.mult, ALU.mult))
            dve.wait_ge(shrunk, 1)
            v.tensor_tensor(flat(A), flat(A), flat(TMP), ALU.mult)
            v.tensor_tensor(flat(K), flat(K), flat(TMP), ALU.mult).then_inc(factors_ready, 1)

            def level(n):
                a = CONSTS["level"][0] + n * C
                return over(consts[:, a:a + C], CM)

            def bank6(b):
                return banks[:, b, 0:CM * C].rearrange("p (c v) -> p c v", c=CM)

            nl = nd = 0
            dve.wait_ge(factors_ready, 1)
            for grp in groups:
                if nl:
                    dve.wait_ge(inv_x, nl + nd)
                for i, j in enumerate(grp):
                    nl += 1
                    dve.wait_ge(inv_l, nl)
                    link(v.tensor_tensor(xt_all[j], bank6(4 * i + 1), over(const("level0_t"), CM), ALU.mult))
                    v.tensor_tensor(xt_all[j], xt_all[j], over(const("ids"), CM), ALU.add)
                    dve.wait_ge(inv_lsb, nl)
                    v.tensor_tensor(inv_bufs[i][1], inv_bufs[i][0], level(1), ALU.mult).then_inc(inv_x, 1)
                for lev in range(1, levels(grp[0])):
                    for i, j in enumerate(grp):
                        nd += 1
                        if lev + 1 < levels(j):
                            dve.wait_ge(inv_y, nd)
                            v.tensor_tensor(inv_bufs[i][1], inv_bufs[i][0], level(lev + 1), ALU.mult)
                        dve.wait_ge(inv_d, nd)
                        v.tensor_tensor(xt_all[j], bank6(4 * i + 2), xt_all[j], ALU.add).then_inc(inv_x, 1)
            dve.wait_ge(s0_t, CM)

            def mask_batches(src, out=masked):
                inb = const("in_batch").rearrange("p (b t) -> p b t", b=NB)
                for c in range(CM):
                    ins = v.tensor_tensor(masked[:, c], src[:, c, TP:T].unsqueeze(1).broadcast_to([P, NB, C]), inb, ALU.mult)
                ins.then_inc(masked_ready, 1)

            def mask_rows(src):
                for c in range(CM):
                    ins = v.tensor_tensor(masked[:, c], over(src[:, c, :], NB), each(const("of_batch"), HD), ALU.mult)
                ins.then_inc(masked_ready, 1)

            def intra_of(n):
                s = order[n] == SAMPLE
                for m, name in enumerate(("before", "upto", "upto")):
                    dve.wait_ge(intra, 3 * n + m + 1)
                    v.tensor_tensor(prep[n % 2][3 + m], bank6(3 + m), over(const(name + ("_s" if s else "")), CM),
                                    ALU.mult).then_inc(intra_out, 1)

            def centre(n):
                o = o_buf[n % 2]
                dve.wait_ge(o_sb, n + 1)
                link(v.tensor_reduce(small[:, 6:12], o, AX_X, ALU.add))
                link(v.tensor_scalar(small[:, 12:18], small[:, 6:12], -1.0 / HD, None, ALU.mult))
                link(v.tensor_tensor(o_centred, o, each(small[:, 12:18], HD), ALU.add))
                link(v.tensor_tensor(on_buf[n % 2], o_centred, o_centred, ALU.mult))
                v.tensor_reduce(small[:, 18:24], on_buf[n % 2], AX_X, ALU.add).then_inc(var_ready, 1)

            def scale_outputs(n):
                dve.wait_ge(gn_ready, n + 1)
                v.tensor_tensor(on_buf[n % 2], o_centred, each(small[:, 30:36], HD), ALU.mult).then_inc(on_ready, 1)

            mask_batches(KK)
            intra_of(0)
            for n, j in enumerate(order):
                if not n:
                    dve.wait_ge(u_psum, 1)
                    mask_batches(R)
                    dve.wait_ge(o_psum, 1)
                    dve.wait_ge(sa_sb, 1)
                    mask_rows(sa_buf)
                    for m in range(2 * CM):
                        if m == CM:
                            dve.wait_ge(dsm_psum, CM)
                            mask_rows(prep[0][2])
                        dve.wait_ge(dsm_psum, m + 1)
                        s = s0t[:, m % CM].rearrange("p b v -> p (b v)")
                        ins = v.tensor_tensor(s, banks[:, 4 + m % 2, :], s, ALU.add)
                        ins.then_inc(dsm_free, 1)
                    dve.wait_ge(dsm_free, 2 * CM)
                    for c in range(CM):
                        ins = v.tensor_tensor(s0t[:, c], s0t[:, c], each(decay_end[:, c, 8:16], HD), ALU.mult)
                    ins.then_inc(s0_scaled, 1)
                    centre(0)
                    dve.wait_ge(st_t, CM)
                    intra_of(1)
                else:
                    scale_outputs(n - 1)
                    if n + 1 < NCH:
                        intra_of(n + 1)
                    dve.wait_ge(ds_psum, n)
                    after = state[:, (n + 1) % 2]
                    link(v.tensor_tensor(after, bank6(6), state[:, n % 2], ALU.add))
                    v.tensor_tensor(after, after, each(decay_end[:, :, j], HD), ALU.mult).then_inc(s_new, 1)
                    centre(n)
            scale_outputs(NCH - 1)
            dve.wait_ge(turned_out, 4 * NCH)
            cat0 = att[0]["cat"]
            for c in range(CM):
                ins = v.tensor_scalar(R[:, c, :], R[:, c, :], vec[:, c, LNX_W:LNX_W + 1], vec[:, c, LNX_B:LNX_B + 1], ALU.mult, ALU.add)
            link(ins)
            link(v.tensor_tensor(flat(R), flat(R), flat(BON), ALU.add))
            v.tensor_tensor(flat(cat0[:, 0:CM, :]), flat(R), flat(G), ALU.mult).then_inc(cat_ready, 1)

            def spread_queries(dst, src):
                link(v.memset(dst, 0.0))
                for c in range(2):
                    for i in range(2):
                        hd = 2 * c + i
                        ins = v.tensor_copy(dst[hp(i), :, c, hd * TS:(hd + 1) * TS],
                                            src[hp(i), c, TP:T].rearrange("p (b t) -> p b t", b=NB))
                return ins

            def maxima(l, q, kind, x, hd):
                w = WIDTH[kind]
                s, m = score_banks(q, kind), stat(q, 2, kind)
                dve.wait_ge(sm_s, q + 1)
                if q >= 3:
                    dve.wait_ge(sm_exp, q - 2)
                if kind == "dil_p":
                    link(v.tensor_tensor_reduce(s, s, mask_p[:, x, :], 1.0, -3e38, ALU.add, ALU.max, m))
                elif kind == "dil_s":
                    link(v.tensor_tensor(s[:, 1152:w], s[:, 1152:w], mask_new[:, x, :], ALU.add))
                    link(v.tensor_tensor(s[:, 0:1152], s[:, 0:1152], mask_cached, ALU.add))
                    link(v.tensor_reduce(m, s, AX_X, ALU.max))
                else:
                    link(v.tensor_reduce(m, s, AX_X, ALU.max))
                v.tensor_scalar(stat(q, 0, kind), m, -SCALE, None, ALU.mult).then_inc(sm_max, 1)

            def normalise(l, q, kind):
                p = probs(l, q, kind)
                dve.wait_ge(sm_exp, q + 1)
                link(v.reciprocal(stat(q, 3, kind), stat(q, 1, kind)))
                v.tensor_scalar(p, p, stat(q, 3, kind), None, ALU.mult).then_inc(sm_p, 1)

            def attention(l, q0):
                for n, st in enumerate(steps[l]):
                    maxima(l, q0 + n, *st)
                    normalise(l, q0 + n, st[0])

            spread_queries(att[0]["qs"][0], qmem[:, :, :]).then_inc(qs_ready, 1)
            attention(0, 0)

            nsplit, nx, ns = [0], [0], [0]

            def low_weights():
                s = nsplit[0]
                nsplit[0] += 1
                n = split_at[s]
                _, nk, w, _, _ = units[n]
                hi, lo = [p[:, 0:nk * w] for p in w_parts[s % 2]]
                dve.wait_ge(w_hi, s + 1)
                v.tensor_tensor(lo, ring[:, n % RING, 0:nk * w], hi.bitcast(F32), ALU.subtract).then_inc(w_lo, 1)

            def low_input(src, k):
                nx[0] += 1
                dve.wait_ge(x_hi, nx[0])
                v.tensor_tensor(x_parts[1][:, k, :], src[:, k, :], x_parts[0][:, k, :].bitcast(F32), ALU.subtract).then_inc(x_lo, 1)

            def scaled_input(norm, g):
                dve.wait_ge(rstd_ready, norm + 1)
                for k in range(KD):
                    v.scalar_tensor_tensor(y[:, k, :], h[:, k, :], vec[:, k, g:g + 1], rstd, ALU.mult, ALU.mult).then_inc(x_scaled, 1)
                    if k:
                        low_input(y, k - 1)
                low_input(y, KD - 1)

            def add_normed(norm, g):
                dve.wait_ge(rstd_ready, norm + 1)
                for k in range(KD + 1):
                    if k < KD:
                        ns[0] += 1
                        v.scalar_tensor_tensor(y[:, k, :], y[:, k, :], vec[:, k, g:g + 1], rstd, ALU.mult, ALU.mult).then_inc(y_scaled, 1)
                    if k:
                        dve.wait_ge(y_scaled, ns[0] - (1 if k < KD else 0))
                        v.tensor_tensor(h[:, k - 1, :], h[:, k - 1, :], y[:, k - 1, :], ALU.add).then_inc(h_ready, 1)

            def mix_out(src, nk):
                low_weights()
                for k in range(nk):
                    low_input(src, k)
                for _ in range(3):
                    low_weights()

            def feed_forward(l, norm):
                dve.wait_ge(h_back, 16 * (l + 1))
                add_normed(norm, G_POST + l)
                low_weights()
                dve.wait_ge(h_ready, KD * (2 * l + 1))
                scaled_input(norm + 1, G_PRE_F + l)
                for half in range(2):
                    for u in range(half * HF, (half + 1) * HF):
                        low_weights()
                        dve.wait_ge(tile_free, ffn_in_end[KF * l + u])
                        g = gate[:, u % 2, :]
                        hi, lo = [x[:, u - half * HF, :] for x in f_parts]
                        link(v.tensor_tensor(g, g, up[:, u % 2, :], ALU.mult))
                        link(v.tensor_copy(hi, g))
                        v.tensor_tensor(lo, g, hi.bitcast(F32), ALU.subtract).then_inc(f_ready, 1)
                    for c in range(KD):
                        if not (half and c == KD - 1):
                            low_weights()
                        if half:
                            dve.wait_ge(tile_free, ffn_in_end[KF * (l + 1) - 1] + c + 1)
                            v.tensor_tensor(y[:, c, :], y[:, c, :], up[:, c % 2, :], ALU.add).then_inc(y_added, 1)
                dve.wait_ge(y_added, KD * (l + 1))
                add_normed(norm + 2, G_POST_F + l)

            mix_out(att[0]["cat"], KD)
            feed_forward(0, 1)
            low_weights()
            dve.wait_ge(h_ready, 2 * KD)
            scaled_input(4, G_KV)
            for _ in range(6):
                low_weights()
            dve.wait_ge(tile_ready, END_KV)
            scaled_input(4, G_PRE + 1)
            for _ in range(3):
                low_weights()
            dve.wait_ge(cos_in, 16)
            for n, x in enumerate((kc, qc)):
                dve.wait_ge(tile_free, END_QKV + CM * (n + 1))
                v.tensor_tensor(x, x, over(cos_sin[:, 0, :], CM), ALU.mult)
                link(v.tensor_tensor(rot[n], rot[n], over(cos_sin[:, 1, :], CM), ALU.mult))
                v.tensor_tensor(x, x, rot[n], ALU.add).then_inc(rotated, 1)
            dve.wait_ge(rotated, 2)
            dve.wait_ge(sm_pt, NT0 + 15 + 4)
            dve.wait_ge(h_saved, 32)
            for g in range(3):
                spread_queries(att[1]["qs"][1 + g], qc[:, 2 * g:2 * g + 2, :])
            spread_queries(att[1]["qs"][0], qmem[:, :, :]).then_inc(qs_ready, 1)
            v.tensor_copy(v_tok, kv_tok[:, :, 1, 0:256])
            v.tensor_copy(v_new, kv_new[:, 1, :].rearrange("p (g n) -> p g n", g=3)).then_inc(v_copied, 1)
            dve.wait_ge(masks_in, 48)
            attention(1, len(steps[0]))
            mix_out(att[1]["cat"], 4)
            feed_forward(1, 5)


_OUTS = [(1, TP, D), (NB, TS, D), (1, 1, 12, HD, HD), (1, 1, D), (1, 128, 2, 4, HD), (1, 512, 2, 4, HD),
         (1, 1024, 2, 4, HD), (2, 1, 256, 2, 4, HD), (1, NB, 12, HD, HD), (1, NB, D), (NB, 128, 2, 4, HD),
         (NB, 512, 2, 4, HD), (NB, 1024, 2, 4, HD)]
_UNUSED = ("a_v0", "a_v1", "a_v2")


def constants():
    import numpy as np

    f = np.float32
    p = np.arange(P)
    out = np.zeros((P, NCONST), f)

    def put(name, v):
        a, b = CONSTS[name]
        out[:, a:b] = v

    put("ident", np.eye(P))
    put("mean", np.full((P, P), 1.0 / D))
    put("pair", p[:, None] // HD == p[None] // HD)
    swap = np.zeros((P, P))
    for to in range(P):
        d = to % HD
        swap[to + HD // 2 if d < HD // 2 else to - HD // 2, to] = -1.0 if d < HD // 2 else 1.0
    put("swap", swap)
    t = np.arange(T)
    put("carry", np.broadcast_to(np.where(t < TP, t % C != 0, (t - TP) % TS != 0), (P, T)))
    s, q = (p % C)[:, None], np.arange(C)[None]
    put("before", s < q)
    put("upto", s <= q)
    put("before_s", (s < q) & (s // TS == q // TS))
    put("upto_s", (s <= q) & (s // TS == q // TS))
    put("level", np.concatenate([(((s >> n) & 1) == 1) & ((q >> n) == (s >> n) - 1) for n in range(LEVELS)], 1))
    put("level0_t", ((q & 1) == 1) & (s == q - 1))
    put("ids", s == q)
    put("in_batch", np.broadcast_to((np.arange(NB)[:, None] == (np.arange(C) // TS)[None]).reshape(-1), (P, NB * C)))
    put("of_batch", s // TS == np.arange(NB)[None])
    put("eps", 1e-6)
    put("lnx_eps", HD * 1e-5)
    put("ln_shift", 10 * np.log(2.0))

    half = HD // 2
    inv = f(10000.0) ** (-np.arange(half, dtype=f) / f(half))
    pos = np.concatenate([np.arange(TP), 1024 + np.tile(np.arange(TS), NB)]).astype(f)
    ang = pos[:, None] * inv[None]
    cs = np.stack([np.cos(ang), np.sin(ang)], 0).astype(f)
    cos_sin = np.ascontiguousarray(cs.transpose(2, 0, 1)[p % half])

    def bias(ok):
        return np.where(ok, 0.0, NEG).astype(f)

    r = np.arange(4)[None, :, None]
    off = (4 * p[:, None, None] + r) - np.arange(TP)[None, None]
    g0 = bias((off >= 0) & (off <= 128))
    du = p[:, None] - p[None]
    same = np.concatenate([bias(du >= 0), bias((du >= 0) & (du % 4 == 0))], 1)
    mask_p = np.concatenate([g0, np.broadcast_to(same[:, None], (P, 4, 2 * P))], 2)
    row = np.arange(64)
    tq, bq = (row % TS)[:, None], (row // 32)[:, None]
    k1, k0, k2 = np.arange(512)[None], np.arange(128)[None], np.arange(512)[None]
    parts = [bias((k1 >= tq) & ((k1 - tq) % 4 == 0)), bias((k2 % TS == tq) & (k2 >= 0)), bias(k0 >= tq)]
    new = np.arange(NS)[None]
    for g in range(NB // 2):
        for dil in (1, 4, 16):
            d = tq - new % TS
            parts.append(bias((new // TS == 2 * g + bq) & (d >= 0) & (d % dil == 0)))
    new_rows = np.stack([np.concatenate(parts[3 + 3 * g:6 + 3 * g], 1) for g in range(NB // 2)], 1)
    return {"consts": out, "cos_sin": cos_sin, "mask_p": mask_p.astype(f),
            "mask_cached": np.concatenate(parts[:3], 1).astype(f), "mask_new": new_rows.astype(f)}


def kernel(**inputs):
    import numpy as np
    import concourse.bacc as bacc
    from concourse.bass_utils import run_bass_kernel_spmd

    nc = bacc.Bacc("TRN2", target_bir_lowering=False, num_devices=1)
    arrays, ins = {}, {}
    given = {n: a for n, a in inputs.items() if n not in _UNUSED}
    for name, a in {**given, **constants()}.items():
        a = np.ascontiguousarray(a)
        arrays[f"in_{name}"] = a
        ins[name] = nc.dram_tensor(f"in_{name}", a.shape, mybir.dt.from_np(a.dtype), kind="ExternalInput").ap()
    outs = [nc.dram_tensor(f"out_{i}", s, F32, kind="ExternalOutput").ap() for i, s in enumerate(_OUTS)]
    trunk(nc, ins, outs)
    r = run_bass_kernel_spmd(nc, [arrays], core_ids=[0])
    return tuple(r.results[0][f"out_{i}"] for i in range(len(_OUTS)))
```
